# Optimizing a Trainium2 kernel written in Bass

```python
import functools
import jax, jax.numpy as jnp
from jax import lax
import numpy as np

D_MODEL = 1024
BATCH = 1
SEQ = 1024
DEPTH = 1
DEC_BATCH = 8
DEC_SEQ = 1
PAST_LEN = 512
PAGE_SIZE = 128

HEAD_DIM = 64
DIL_GROUPS = ((128, 1), (512, 4), (2048, 16))
HEADS_PER_GROUP = 4
N_ATTN_HEADS = HEADS_PER_GROUP * len(DIL_GROUPS)
ATTN_W = N_ATTN_HEADS * HEAD_DIM
ATTN_OUT_W = HEADS_PER_GROUP * HEAD_DIM
STRIDE_STEPS = 128
CHUNK = 128
SG_GROUPS = 4
SG_GROUP_W = 128
SG_W = SG_GROUPS * SG_GROUP_W
D_FF = -(-8 * D_MODEL // (3 * 256)) * 256
IN_W = 3 * ATTN_W + 2 * SG_W + 2 * D_MODEL
EPS = 1e-6
SCALE = HEAD_DIM ** -0.5
NEG = -1e30

kernel_name = 'gated_dilated_attn_gmlp_decoder_step'

def _rmsnorm(x, g):
    xf = x.astype(jnp.float32)
    y = xf * lax.rsqrt(jnp.mean(xf * xf, axis=-1, keepdims=True) + EPS)
    return (y * g.astype(jnp.float32)).astype(x.dtype)

def _layernorm(x, g, b):
    xf = x.astype(jnp.float32)
    mu = jnp.mean(xf, axis=-1, keepdims=True)
    xc = xf - mu
    y = xc * lax.rsqrt(jnp.mean(xc * xc, axis=-1, keepdims=True) + EPS)
    return (y * g.astype(jnp.float32) + b.astype(jnp.float32)).astype(x.dtype)

def _to_residue(a, dil):
    n, s = a.shape[:2]
    rest = a.shape[2:]
    return a.reshape(n, s // dil, dil, *rest).swapaxes(1, 2).reshape(n * dil, s // dil, *rest)

def _from_residue(a, dil, n):
    m = a.shape[1]
    rest = a.shape[2:]
    return a.reshape(n, dil, m, *rest).swapaxes(1, 2).reshape(n, m * dil, *rest)

def _band_attn(q, k, v):
    n, L, H, hd = q.shape
    blk = STRIDE_STEPS
    nb = -(-L // blk)
    pad = nb * blk - L
    qb = jnp.pad(q, ((0, 0), (0, pad), (0, 0), (0, 0))).reshape(n, nb, blk, H, hd)

    def two_blocks(a):
        ab = jnp.pad(a, ((0, 0), (blk, pad), (0, 0), (0, 0))).reshape(n, nb + 1, blk, H, hd)
        return jnp.concatenate([ab[:, :-1], ab[:, 1:]], axis=2)

    kw, vw = two_blocks(k), two_blocks(v)
    s = jnp.einsum('nbqhd,nbkhd->nbhqk', qb, kw).astype(jnp.float32) * SCALE
    qi = jnp.arange(blk)[:, None]
    ki = jnp.arange(2 * blk)[None, :]
    dist = qi + blk - ki
    kpos = jnp.arange(nb)[:, None, None] * blk - blk + ki[None]
    valid = ((dist >= 0) & (dist <= blk))[None] & (kpos >= 0)
    s = jnp.where(valid[None, :, None], s, NEG)
    lse = jax.nn.logsumexp(s, axis=-1)
    p = jnp.exp(s - lse[..., None])
    o = jnp.einsum('nbhqk,nbkhd->nbqhd', p.astype(v.dtype), vw).reshape(n, nb * blk, H, hd)[:, :L]
    lse = lse.transpose(0, 1, 3, 2).reshape(n, nb * blk, H)[:, :L]
    return o, lse

def _merge_groups(outs, lses):
    o = jnp.stack(outs, 0).astype(jnp.float32)
    w = jax.nn.softmax(jnp.stack(lses, 0), axis=0)
    y = jnp.sum(w[..., None] * o, axis=0)
    return y.reshape(y.shape[0], y.shape[1], ATTN_OUT_W).astype(outs[0].dtype)

def _dilated_prompt(q, k, v):
    n, s = q.shape[:2]
    outs, lses, rows = [], [], []
    for gi, (win, dil) in enumerate(DIL_GROUPS):
        hs = slice(gi * HEADS_PER_GROUP, (gi + 1) * HEADS_PER_GROUP)
        qg, kg, vg = q[:, :, hs], k[:, :, hs], v[:, :, hs]
        o, lse = _band_attn(_to_residue(qg, dil), _to_residue(kg, dil), _to_residue(vg, dil))
        outs.append(_from_residue(o, dil, n))
        lses.append(_from_residue(lse, dil, n))
        keep = min(win, s)
        rows.append(jnp.stack([kg[:, s - keep:], vg[:, s - keep:]], axis=2))
    return _merge_groups(outs, lses), rows

def _dilated_sample(q, k, v, bufs):
    t = q.shape[1]
    outs, lses, rows = [], [], []
    for gi, (win, dil) in enumerate(DIL_GROUPS):
        hs = slice(gi * HEADS_PER_GROUP, (gi + 1) * HEADS_PER_GROUP)
        qg, kg, vg = q[:, :, hs], k[:, :, hs], v[:, :, hs]
        buf = bufs[gi]
        L = buf.shape[1]
        kc = jnp.concatenate([buf[:, :, 0].astype(kg.dtype), kg], axis=1)
        vc = jnp.concatenate([buf[:, :, 1].astype(vg.dtype), vg], axis=1)
        idx = L + jnp.arange(t)[:, None] - jnp.arange(STRIDE_STEPS + 1)[None, :] * dil
        valid = idx >= 0
        idxc = jnp.maximum(idx, 0)
        kgat = jnp.take(kc, idxc, axis=1)
        vgat = jnp.take(vc, idxc, axis=1)
        s = jnp.einsum('nthd,ntkhd->nthk', qg, kgat).astype(jnp.float32) * SCALE
        s = jnp.where(valid[None, :, None, :], s, NEG)
        lse = jax.nn.logsumexp(s, axis=-1)
        p = jnp.exp(s - lse[..., None])
        outs.append(jnp.einsum('nthk,ntkhd->nthd', p.astype(vg.dtype), vgat))
        lses.append(lse)
        rows.append(jnp.stack([kg, vg], axis=2))
    return _merge_groups(outs, lses), rows

def _spatial_mix(vs, w_sg, b_sg):
    n, t, _ = vs.shape
    nc = -(-t // CHUNK)
    pad = nc * CHUNK - t
    vb = jnp.pad(vs, ((0, 0), (0, pad), (0, 0))).reshape(n, nc, CHUNK, SG_GROUPS, SG_GROUP_W)
    w = w_sg * jnp.tril(jnp.ones((CHUNK, CHUNK), w_sg.dtype))
    mixed = jnp.einsum('gts,ncsgd->nctgd', w, vb) + b_sg.T[None, None, :, :, None]
    return mixed.reshape(n, nc * CHUNK, SG_W)[:, :t]

def _layer(x, core, g_mp, g_mq, g_fp, g_fq, w_in, lvg, lvb, w_sg, b_sg, w_pa, w_pb, w_o, w_g, w_u, w_d):
    n, t, _ = x.shape
    h = _rmsnorm(x, g_mp)
    z = h @ w_in
    a = ATTN_W
    splits = [a, 2 * a, 3 * a, 3 * a + SG_W, 3 * a + 2 * SG_W, 3 * a + 2 * SG_W + D_MODEL]
    q, k, v, u, vs, ga, gb = jnp.split(z, splits, axis=-1)
    q = q.reshape(n, t, N_ATTN_HEADS, HEAD_DIM)
    k = k.reshape(n, t, N_ATTN_HEADS, HEAD_DIM)
    v = v.reshape(n, t, N_ATTN_HEADS, HEAD_DIM)
    o_a, rows = core(q, k, v)
    vs = _layernorm(jax.nn.gelu(vs), lvg, lvb)
    o_b = jax.nn.gelu(u) * _spatial_mix(vs, w_sg, b_sg)
    m = jax.nn.sigmoid(ga) * (o_a @ w_pa) + jax.nn.sigmoid(gb) * (o_b @ w_pb)
    x = x + _rmsnorm(m @ w_o, g_mq)
    h = _rmsnorm(x, g_fp)
    f = (jax.nn.silu(h @ w_g) * (h @ w_u)) @ w_d
    x = x + _rmsnorm(f, g_fq)
    return x, rows, vs

def setup_inputs(seed: int = 0) -> dict:
    key = jax.random.key(seed)
    ks = jax.random.split(key, 24)
    f32 = jnp.float32

    def nrm(k, shape, scale):
        return jax.random.normal(k, shape, f32) * scale

    def gain(k, shape):
        return 1.0 + 0.05 * jax.random.normal(k, shape, f32)

    cache_len = [min(w, PAST_LEN) for (w, _) in DIL_GROUPS]
    return {
        'x_prompt': nrm(ks[0], (BATCH, SEQ, D_MODEL), 1.0),
        'x_sample': nrm(ks[1], (DEC_BATCH, DEC_SEQ, D_MODEL), 1.0),
        'cache_win0': nrm(ks[2], (DEPTH, DEC_BATCH, cache_len[0], 2, HEADS_PER_GROUP, HEAD_DIM), 1.0),
        'cache_win1': nrm(ks[3], (DEPTH, DEC_BATCH, cache_len[1], 2, HEADS_PER_GROUP, HEAD_DIM), 1.0),
        'cache_win2': nrm(ks[4], (DEPTH, DEC_BATCH, cache_len[2], 2, HEADS_PER_GROUP, HEAD_DIM), 1.0),
        'g_mix_pre': gain(ks[5], (DEPTH, D_MODEL)),
        'g_mix_post': gain(ks[6], (DEPTH, D_MODEL)),
        'g_ffn_pre': gain(ks[7], (DEPTH, D_MODEL)),
        'g_ffn_post': gain(ks[8], (DEPTH, D_MODEL)),
        'w_in': nrm(ks[9], (DEPTH, D_MODEL, IN_W), D_MODEL ** -0.5),
        'ln_v_g': gain(ks[10], (DEPTH, SG_W)),
        'ln_v_b': nrm(ks[11], (DEPTH, SG_W), 0.02),
        'w_sg': nrm(ks[12], (DEPTH, SG_GROUPS, CHUNK, CHUNK), 0.5 * CHUNK ** -0.5),
        'b_sg': 1.0 + nrm(ks[13], (DEPTH, SG_GROUPS, CHUNK), 0.1),
        'w_proj_attn': nrm(ks[14], (DEPTH, ATTN_OUT_W, D_MODEL), ATTN_OUT_W ** -0.5),
        'w_proj_sg': nrm(ks[15], (DEPTH, SG_W, D_MODEL), SG_W ** -0.5),
        'w_out': nrm(ks[16], (DEPTH, D_MODEL, D_MODEL), D_MODEL ** -0.5),
        'w_gate': nrm(ks[17], (DEPTH, D_MODEL, D_FF), D_MODEL ** -0.5),
        'w_up': nrm(ks[18], (DEPTH, D_MODEL, D_FF), D_MODEL ** -0.5),
        'w_down': nrm(ks[19], (DEPTH, D_FF, D_MODEL), D_FF ** -0.5),
    }

def reference(x_prompt, x_sample, cache_win0, cache_win1, cache_win2, g_mix_pre, g_mix_post, g_ffn_pre, g_ffn_post, w_in, ln_v_g, ln_v_b, w_sg, b_sg, w_proj_attn, w_proj_sg, w_out, w_gate, w_up, w_down):
    yp, ys = x_prompt, x_sample
    rows_p = [[], [], []]
    rows_s = [[], [], []]
    sg_rows = []
    for l in range(DEPTH):
        lw = (g_mix_pre[l], g_mix_post[l], g_ffn_pre[l], g_ffn_post[l], w_in[l], ln_v_g[l], ln_v_b[l],
              w_sg[l], b_sg[l], w_proj_attn[l], w_proj_sg[l], w_out[l], w_gate[l], w_up[l], w_down[l])
        yp, rp, _ = _layer(yp, _dilated_prompt, *lw)
        core_s = functools.partial(_dilated_sample, bufs=(cache_win0[l], cache_win1[l], cache_win2[l]))
        ys, rs, vs_s = _layer(ys, core_s, *lw)
        for gi in range(len(DIL_GROUPS)):
            rows_p[gi].append(rp[gi])
            rows_s[gi].append(rs[gi])
        sg_rows.append(vs_s)
    return (yp, ys,
            jnp.stack(rows_p[0]), jnp.stack(rows_p[1]), jnp.stack(rows_p[2]),
            jnp.stack(rows_s[0]), jnp.stack(rows_s[1]), jnp.stack(rows_s[2]),
            jnp.stack(sg_rows))


_drawn_inputs = setup_inputs


def setup_inputs(seed=0):
    import zlib

    import numpy as np

    out = dict(_drawn_inputs(seed))
    spreads = {}
    factors = {'ln_v_b': 2.759}
    for name, (base, spread) in spreads.items():
        noise = np.random.default_rng([zlib.crc32(name.encode()), seed]).standard_normal(out[name].shape)
        drawn = base * np.exp(spread * noise) if base else spread * noise
        out[name] = __import__('jax').numpy.asarray(drawn.astype(out[name].dtype))
    for name, factor in factors.items():
        out[name] = (out[name] * factor).astype(out[name].dtype)
    return out
```

```python
from contextlib import ExitStack

import concourse.bass as bass
from concourse import mybir

ALU = mybir.AluOpType
ACT = mybir.ActivationFunctionType
F32 = mybir.dt.float32
F32R = mybir.dt.float32r
BF16 = mybir.dt.bfloat16
I32 = mybir.dt.int32

P = 128
D = 1024
KD = D // P
SEQ = 1024
NS = 8
NT = SEQ + NS
TG = NT // 3
HD = 64
SLOTS = 4
GROUPS = 3
AW = 768
SGW = 512
FF = 2816
KF = FF // P
U_COL, V_COL = 3 * AW, 3 * AW + SGW
GA_COL = 3 * AW + 2 * SGW
GB_COL = GA_COL + D
DIL = (1, 4, 16)
CKEYS = (128, 128, 32)
EPS = 1e-6
SCALE = HD ** -0.5
NEG = -1e30

STAGES = [("uv", 8, 8), ("qkv0", 9, 9), ("pb", 4, 8), ("gb0", 4, 4), ("qkv1", 9, 9), ("gb1", 4, 4),
          ("ga", 8, 8), ("pa", 2, 8), ("wo", 8, 8), ("ffn", 60, 80), ("tail", 6, 12)]
U0, M0 = {}, {}
_u = _m = 0
for _name, _nu, _nm in STAGES:
    U0[_name], M0[_name] = _u, _m
    _u += _nu
    _m += _nm
UNITS = _u
FG = 4
ROUNDS = KF // FG
NORMS = [("chain", 0, 0), ("chain", 0, 1), ("apply", 0, 0), ("chain", 0, 2), ("apply", 0, 1), ("chain", 1, 0),
         ("apply", 0, 2), ("chain", 1, 1), ("apply", 1, 0), ("chain", 1, 2), ("apply", 1, 1), ("apply", 1, 2)]
LAST_NORM = [("chain", 2, 0), ("chain", 2, 1), ("apply", 2, 0), ("chain", 2, 2), ("apply", 2, 1), ("apply", 2, 2)]


class Steps:

    def __init__(self, eng, sem):
        self.eng, self.sem, self.n, self.term = eng, sem, 0, 0

    def mark(self, ins):
        ins.then_inc(self.sem, 1)
        self.n += 1

    def link(self, ins):
        ins.then_inc(self.sem, 1)
        self.n += 1
        self.eng.wait_ge(self.sem, self.term + self.n)

    def enter(self, i, per):
        self.start, self.per, self.term = self.n, per, i * per

    def leave(self, rounds):
        assert self.n - self.start == self.per, (self.n - self.start, self.per)
        self.n, self.term = self.start + self.per * rounds, 0


def build(nc, A, O):
    ctx = ExitStack()
    sem = lambda name: ctx.enter_context(nc.semaphore(name))
    base = (nc.sbuf_base + 31) // 32 * 32
    RB = KD * NT * 4
    R = [base + RB * i for i in range(5)]
    W = base + 5 * RB
    R4 = base + 4 * RB
    X = R4 + RB
    W = nc.sbuf_usable_end // 32 * 32 - 6 * 4096
    XEND = W

    def at(name, shape, dt, off):
        n = 4 if dt in (F32, F32R, I32) else 2
        for s in shape[1:]:
            n *= s
        assert off + n <= nc.sbuf_usable_end, (name, off, n)
        return nc.alloc_sbuf_tensor_at(name, shape, dt, offset=off), off + (n + 31) // 32 * 32

    with ctx:
        w_raw = [at(f"w_raw{i}", [P, 8 * P], F32, W + 4096 * i)[0] for i in range(2)]
        w_hi = [at(f"w_hi{i}", [P, 8 * P], F32R, W + 4096 * (2 + i))[0] for i in range(2)]
        w_lo = [at(f"w_lo{i}", [P, 8 * P], F32R, W + 4096 * (4 + i))[0] for i in range(2)]
        h_hi, _ = at("h_hi", [P, KD, NT], F32R, R[0])
        h_lo, _ = at("h_lo", [P, KD, NT], F32R, R[1])
        xT, _ = at("xT", [P, KD, NT], F32, R[0])
        oa_hi, _o = at("oa_hi", [P, 2, NT], F32R, R[1])
        oa_lo, _o = at("oa_lo", [P, 2, NT], F32R, _o)
        pt, _o = at("pt", [P, 4, TG], F32, _o)
        f_hi, _ = at("f_hi", [P, KD, NT], F32R, R[1])
        mb, _ = at("mb", [P, KD, NT], F32, R[2])
        m_hi, _ = at("m_hi", [P, KD, NT], F32R, R[2])
        f_lo, _ = at("f_lo", [P, KD, NT], F32R, R[2])
        uv, _ = at("uv", [P, 8, NT], F32, R[3])
        ob_hi, _o = at("ob_hi", [P, 4, NT], F32R, R[3])
        ob_lo, _ = at("ob_lo", [P, 4, NT], F32R, _o)
        m_lo, _ = at("m_lo", [P, KD, NT], F32R, R[3])
        y2, _ = at("y2", [P, KD, NT], F32, R[3])
        g_pre, _o = at("g_pre", [P, D], F32, R[2])
        lnvg, _o = at("lnvg", [P, SGW], F32, _o)
        lnvb, _o = at("lnvb", [P, SGW], F32, _o)
        bsg, _o = at("bsg", [P, 4, P], F32, _o)
        wsg, _o = at("wsg", [P, 4, P], F32, _o)
        wsT, _o = at("wsT", [P, 4, P], F32, _o)
        vc, _o = at("vc", [P, 4, P], F32, _o)
        vt, _o = at("vt", [P, SGW], F32, _o)
        mixt, _o = at("mixt", [P, 4, P], F32, _o)
        w00, _o = at("w00", [NS, 8], F32, _o)
        vw, _o = at("vw", [NS, SGW], F32, _o)
        iot, _o = at("iot", [P, 256], I32, _o)
        iom, _o = at("iom", [P, 256], I32, _o)
        gpack, _o = at("gpack", [24, P], F32, _o)
        assert _o <= R[3]
        oaT, _o = at("oaT", [P, 2, NT], F32, R[3])
        pr, _o = at("pr", [P, 2, 1152], F32, _o)
        prT, _o = at("prT", [P, 9, P], F32, _o)
        qst, _o = at("qst", [P, 2, 2, GROUPS, P], F32, _o)
        otok, _o = at("otok", [P, 2, P], F32, _o)
        gt, _o = at("gt", [P, 2, TG], F32, _o)
        m_now, _o = at("m_now", [P, 4, P], BF16, _o)
        assert _o <= R[4]
        cv, _o = at("cv", [P, 24, 256], F32, R[3] + 2 * NT * 4)
        assert _o <= R[4]
        qk, _o = at("qk", [P, 6, NT], F32, R4)
        vtok, _o = at("vtok", [P, 25, P], F32, _o)
        kst, _ = at("kst", [P, 16, P], F32, _o)
        vT, VTO = at("vT", [P, GROUPS, NT], F32, _o)
        ga, _ = at("ga", [P, KD, NT], F32, R4)
        y1, _ = at("y1", [P, KD, NT], F32, R4)
        a_hi, _o = at("a_hi", [P, FG, NT], F32R, R4)
        a_lo, _ = at("a_lo", [P, FG, NT], F32R, _o)
        xin = [at(f"xin{i}", [P, D], F32, R4 + 4096 * i)[0] for i in range(8)]
        xins, _ = at("xins", [P, D], F32, X)
        m_main, _o = at("m_main", [P, 7, P], BF16, VTO)
        m_edge, _o = at("m_edge", [P, 32, 7], BF16, _o)
        m_far, _o = at("m_far", [P, 2, 256], BF16, _o)
        e_now, _o = at("e_now", [P, 32, 4], BF16, _o)
        ident, _o = at("ident", [P, P], F32, _o)
        ones, _o = at("ones", [P, P], F32, _o)
        gains, _o = at("gains", [P, 3, KD], F32, _o)
        sqkv, _o = at("sqkv", [P, 2, 9, NS], F32, _o)
        stat, _o = at("stat", [P, 64], F32, _o)
        assert _o <= XEND, (_o, XEND)
        kraw, _o = at("kraw", [P, 4, 256], F32, X)
        kcT, _o = at("kcT", [P, 2, 256], F32, _o)
        qz, _o = at("qz", [P, 2, 3, NS, 2], F32, _o)
        sst, _o = at("sst", [P, 2, 96], F32, _o)
        ssr, _o = at("ssr", [32, 320], F32, _o)
        spT, _o = at("spT", [P, 6, 32], F32, _o)
        smask, _o = at("smask", [32, 3, NS], F32, _o)
        svt, _o = at("svt", [NS, 3, 2, 256], F32, _o)
        assert _o <= VTO, (_o, VTO)
        nt_, _ = at("nt_", [P, 3, TG], F32, X)
        sg, _ = at("sg", [P, NT], F32, X + 3 * TG * 4)
        xre, _ = at("xre", [P, 2, D], F32, X)
        acc, _o = at("acc", [P, 3, TG], F32, X + 6 * TG * 4)
        diag, _o = at("diag", [P, 3, P], F32, _o)
        sq, _o = at("sq", [P, 2, TG], F32, _o)
        assert _o <= VTO, (_o, VTO)
        yt, _ = at("yt", [P, 2, D], F32, R4)

        bank = [nc.alloc_psum_tensor(f"bank{i}", [P, 512], F32) for i in range(3)]
        psA = nc.alloc_psum_tensor("psA", [P, 512], F32)
        psB = nc.alloc_psum_tensor("psB", [P, 512], F32)
        psC = nc.alloc_psum_tensor("psC", [P, 512], F32)
        psT = [nc.alloc_psum_tensor(f"psT{i}", [P, 512], F32) for i in range(2)]
        psR = [psA, psB]
        gbank, psO = bank[0:2], bank[2]

        w_in_s = [sem(f"w_landed{i}") for i in range(2)]
        w_hi_s, w_lo_s = sem("w_hi_done"), sem("w_lo_done")
        full = [sem(f"bank_full{i}") for i in range(3)]
        free = [sem(f"bank_free{i}") for i in range(3)]
        dve_s, act_s, pool_s = sem("dve_step"), sem("act_step"), sem("pool_step")
        x_in = [sem(f"x_landed{i}") for i in range(9)]
        gpre_in, small_in, gains_in = sem("g_pre_landed"), sem("small_landed"), sem("gains_landed")
        ident_s, masks_s, gains_t, gains_s = sem("ident_done"), sem("masks_done"), sem("gains_turned"), sem("gains_done")
        x_sq, x_v, x_sd, x_g, x_h, x_t, x_hi, x_lo = [sem("x_" + s) for s in (
            "squared", "var", "sd", "gained", "scaled", "turned", "hi", "lo")]
        uv_s = sem("uv_copied")
        tril_s, ws_t, ws_c = sem("w_sg_masked"), sem("w_sg_turned"), sem("w_sg_copied")
        ln_u, ln_v, ln_t, ln_var, ln_sd, ln_n, ln_mix, ln_o, ln_hi, ln_lo, ln_w, ln_wt = [sem("ln_" + s) for s in (
            "gelu_u", "gelu_v", "turned", "var", "sd", "normalised", "mixed", "gated", "hi", "lo", "weighted", "wturned")]
        sgv_out = sem("sg_v_stored")
        kv_t, kv_d = sem("kv_turned"), sem("kv_stored")
        kv_c = [sem("kv_copied_act"), sem("kv_copied_dve")]
        at_q, at_s, at_m, at_p, at_t0, at_t1, at_c0, at_c1, at_pv, at_o, at_ot, at_oc, at_g, at_gu = [sem("at_" + s) for s in (
            "query", "scores", "max", "probs", "turned0", "turned1", "copied0", "copied1", "pv", "otok", "oturned",
            "ocopied", "tanh", "gated")]
        sk_in = [sem(f"k_cache_landed{i}") for i in range(4)]
        sv_in = sem("v_cache_landed")
        s_qz, s_kt, s_kc, s_sc, s_self, s_sst, s_rows, s_ssr, s_exp, s_pn, s_pt, s_ptc, s_pv, s_oa, s_nt, s_nc, s_out = [
            sem("s_" + s) for s in ("queries", "k_turned", "k_copied", "scores", "self", "scores_out", "rows", "rows_out",
                                    "exp", "probs", "probs_turned", "probs_out", "pv", "o_out", "new_turned", "new_out",
                                    "new_stored")]
        oa_h, oa_s, m_t, m_h, m_l, ga_s = sem("oa_hi"), sem("oa_lo"), sem("m_sum"), sem("m_hi"), sem("m_lo"), sem("ga_tanh")
        xr_in = [sem(f"x_again{i}") for i in range(2)]
        xr_t = sem("x_again_turned")
        xr_c = [sem("x_again_copied_act"), sem("x_again_copied_dve")]
        y1_s, y1_q, y1_a = sem("y1_copied"), sem("y1_squared"), sem("y1_summed")
        n_s, n_v, n_sd, n_d, n_b = sem("norm_sum"), sem("norm_var"), sem("norm_sd"), sem("norm_diag"), sem("norm_spread")
        iota_s, far_s = sem("iota_done"), sem("m_far_started")
        x1_t, x1_s, x1_q, x1_a = sem("x1_term"), sem("x1_done"), sem("x1_squared"), sem("x1_summed")
        f_t, f_h, f_l = sem("f_scaled"), sem("f_hi"), sem("f_lo")
        y2_z, ff_sg, ff_af, ff_h, ff_l = sem("y2_cleared"), sem("ff_silu"), sem("ff_product"), sem("ff_hi"), sem("ff_lo")
        y2_s, y2_q, y2_a = sem("y2_summed"), sem("y2_squared"), sem("y2_sq_summed")
        z_t, z_s, z_turn, z_out = sem("z_term"), sem("z_done"), sem("z_turned"), [sem("z_stored0"), sem("z_stored1")]
        z_c = [sem("z_copied_act"), sem("z_copied_dve")]

        block = ctx.enter_context(nc.Block())
        tgc = [slice(TG * t, TG * t + TG) for t in range(3)]
        NOFF = (0, P, TG - P)
        TILES_OF = (3, 6, 9)

        def chunks(w, r0, kc, c0, width):
            return w[r0:r0 + kc * P, bass.ds(c0, width)].rearrange("(k p) c -> p k c", p=P)

        @block.sync
        def _(sp):
            w_in = A["w_in"][0]

            def load_w(u, par, src, kc):
                if not isinstance(u, int) or u >= 2:
                    sp.wait_ge(w_lo_s, u - 1)
                sp.dma_start(w_raw[par][:].rearrange("p (k c) -> p k c", k=kc), src).then_inc(w_in_s[par], 16)

            xp = A["x_prompt"][0].rearrange("(t p) d -> t p d", p=P)
            xs = A["x_sample"].rearrange("b s d -> (b s) d")
            for t in range(8):
                sp.dma_start(xin[t][:], xp[t]).then_inc(x_in[t], 16)
                if t == 0:
                    sp.dma_start(g_pre[:], A["g_mix_pre"][0:1, :].broadcast_to([P, D])).then_inc(gpre_in, 16)
            sp.dma_start(xins[0:NS, :], xs).then_inc(x_in[8], 16)
            load_w(0, 0, chunks(w_in, 0, 8, U_COL, P), 8)
            load_w(1, 1, chunks(w_in, 0, 8, U_COL + P, P), 8)
            for j, n in enumerate(("g_mix_post", "g_ffn_pre", "g_ffn_post")):
                sp.dma_start(gpack[8 * j:8 * j + 8, :], A[n][0].rearrange("(k p) -> k p", p=P)).then_inc(gains_in, 16)
            sp.dma_start(lnvg[:], A["ln_v_g"][0:1, :].broadcast_to([P, SGW])).then_inc(small_in, 16)
            sp.dma_start(lnvb[:], A["ln_v_b"][0:1, :].broadcast_to([P, SGW])).then_inc(small_in, 16)
            sp.dma_start(bsg[:].rearrange("p g t -> p (g t)"),
                         A["b_sg"].rearrange("l g t -> l (g t)").broadcast_to([P, SGW])).then_inc(small_in, 16)
            sp.dma_start(wsg[:], A["w_sg"][0].rearrange("g t s -> t g s")).then_inc(small_in, 16)
            with nc.allow_non_contiguous_dma("8 x 8 numbers"):
                sp.dma_start(w00[:, 0:4], A["w_sg"][0][:, 0, 0:1].rearrange("g o -> o g").broadcast_to([NS, 4])
                             ).then_inc(small_in, 16)
                sp.dma_start(w00[:, 4:8], A["b_sg"][0][:, 0:1].rearrange("g o -> o g").broadcast_to([NS, 4])
                             ).then_inc(small_in, 16)
            with sp.Fori(1, 4) as i:
                for j in range(2):
                    load_w(2 * i + j, j, chunks(w_in, 0, 8, U_COL + P * (2 * i + j), P), 8)

            def load_qkv(pair):
                for j in range(9):
                    u = U0[f"qkv{pair}"] + j
                    load_w(u, u % 2, chunks(w_in, 0, 8, AW * (j // 3) + 256 * (j % 3) + P * pair, P), 8)

            def store_kv(pair):
                sp.wait_ge(kv_c[0], 6 * (pair + 1))
                sp.wait_ge(kv_c[1], 5 * (pair + 1))
                for g, name in enumerate(("kv_prompt_g0", "kv_prompt_g1", "kv_prompt_g2")):
                    for kv in range(2):
                        dst = O[name][0, 0, :, kv, 2 * pair:2 * pair + 2, :].rearrange("s h d -> s (h d)")
                        src = vtok if kv else kst
                        for half in ((0, 1) if g == 2 else (1,)):
                            for r in range(4):
                                if kv:
                                    tile = 4 + r if g == 0 else 9 + 8 * (g - 1) + 4 * half + r
                                else:
                                    tile = 4 * g + r if g < 2 else 8 + 4 * half + r
                                if g == 0:
                                    sp.dma_start(dst[r:P:4, :], src[96:128, tile, :]).then_inc(kv_d, 16)
                                else:
                                    first = 512 * half if g == 2 else 0
                                    sp.dma_start(dst[first + r:first + 512:4, :], src[:, tile, :]).then_inc(kv_d, 16)

            load_qkv(0)
            for i in range(4):
                u = U0["pb"] + i
                load_w(u, u % 2, chunks(A["w_proj_sg"][0], 0, 4, 256 * i, 256), 4)
                if i == 1:
                    sp.wait_ge(ln_n, 9)
                    sp.dma_start(O["sg_v_sample"][0, :, 0, :], vt[0:NS, :]).then_inc(sgv_out, 16)
            store_kv(0)
            for i in range(4):
                u = U0["gb0"] + i
                load_w(u, u % 2, chunks(w_in, 0, 8, GB_COL + P * i, P), 8)
            load_qkv(1)
            for i in range(4):
                u = U0["gb1"] + i
                load_w(u, u % 2, chunks(w_in, 0, 8, GB_COL + P * (4 + i), P), 8)
                if i == 1:
                    store_kv(1)

            def load_k(kk):
                n, g = kk // 3, kk % 3
                ck, first = CKEYS[g], 0
                rows = A[f"cache_win{g}"][0, n].rearrange("(s r) k h d -> s r k (h d)", r=DIL[g])[:, 0]
                if kk >= 4:
                    sp.wait_ge(s_kt, kk - 3)
                sp.dma_start(kraw[0:ck, kk % 4, :], rows[:, 0, :]).then_inc(sk_in[kk % 4], 16)
                sp.dma_start(cv[0:ck, kk, :], rows[:, 1, :]).then_inc(sv_in, 16)

            for i in range(8):
                u = U0["ga"] + i
                load_w(u, u % 2, chunks(w_in, 0, 8, GA_COL + P * i, P), 8)
                if i == 1:
                    sp.wait_ge(at_oc, 17)
                    sp.wait_ge(at_gu, 26)
                    sp.wait_ge(kv_d, 16 * 64)
                    for kk in range(8):
                        load_k(kk)
                elif 1 < i < 6:
                    for kk in range(4 * i, 4 * i + 4):
                        load_k(kk)
            sp.wait_ge(s_nc, 3)
            for g in range(GROUPS):
                sp.dma_start(O[f"kv_sample_g{g}"][0, :, 0].rearrange("b k h d -> b (k h d)"),
                             svt[:, g].rearrange("b k c -> b (k c)")).then_inc(s_out, 16)
            for i in range(2):
                u = U0["pa"] + i
                load_w(u, u % 2, chunks(A["w_proj_attn"][0], 0, 2, 512 * i, 512), 2)

            def x_again(t):
                if t == 0:
                    sp.wait_ge(s_oa, 2)
                    sp.wait_ge(s_out, 48)
                if t >= 2:
                    sp.wait_ge(xr_t, t - 1)
                rows = P if t < 8 else NS
                sp.dma_start(xre[0:rows, t % 2, :], xp[t] if t < 8 else xs).then_inc(xr_in[t % 2], 16)

            for i in range(8):
                u = U0["wo"] + i
                load_w(u, u % 2, chunks(A["w_out"][0], 0, 8, P * i, P), 8)
                x_again(i)
            wg, wu, wd = A["w_gate"][0], A["w_up"][0], A["w_down"][0]
            x_again(8)
            with sp.Fori(0, ROUNDS) as i:
                for j in range(FG):
                    u = U0["ffn"] + 12 * i + 2 * j
                    load_w(u, 0, chunks(wg, 0, 8, 512 * i + P * j, P), 8)
                    load_w(u + 1, 1, chunks(wu, 0, 8, 512 * i + P * j, P), 8)
                for j in range(4):
                    u = U0["ffn"] + 12 * i + 8 + j
                    load_w(u, j % 2, wd[bass.ds(512 * i, 512), 256 * j:256 * j + 256].rearrange("(k p) c -> p k c", p=P), 4)
            u = U0["tail"]
            for j in range(2):
                load_w(u + 2 * j, 0, chunks(wg, 0, 8, 512 * ROUNDS + P * j, P), 8)
                load_w(u + 2 * j + 1, 1, chunks(wu, 0, 8, 512 * ROUNDS + P * j, P), 8)
            for j in range(2):
                load_w(u + 4 + j, j, chunks(wd, 512 * ROUNDS, 2, 512 * j, 512), 2)
            yp = O["y_prompt"][0].rearrange("(t p) d -> t p d", p=P)
            for t in range(9):
                sp.wait_ge(z_c[0], t + 1)
                sp.wait_ge(z_c[1], t + 1)
                dst = yp[t] if t < 8 else O["y_sample"].rearrange("b s d -> (b s) d")
                sp.dma_start(dst, yt[0:P if t < 8 else NS, t % 2, :]).then_inc(z_out[t % 2], 16)
            sp.wait_ge(z_out[0], 80)
            sp.wait_ge(z_out[1], 64)
            sp.wait_ge(kv_d, 16 * 64)
            sp.wait_ge(s_out, 48)
            sp.wait_ge(sgv_out, 16)

        @block.tensor
        def _(pe):
            mm = nc.tensor.matmul

            def turn(out, in_):
                k = in_.shape[0]
                return nc.tensor.transpose(out, in_, ident[0:k, 0:k])

            def job(m, par, b, tg, kc, width, hi, lo, out=None):
                pe.wait_ge(free[tg], m + 1)
                out = out or bank[tg]
                n = 0
                for k in range(kc):
                    ws = slice(width * k + P * b, width * k + P * b + P)
                    for w, x in ((w_hi, hi), (w_hi, lo), (w_lo, hi)):
                        ins = mm(out[:, 0:TG], w[par][:, ws], x[:, k, tgc[tg]], start=(n == 0), stop=(n == 3 * kc - 1))
                        n += 1
                return ins.then_inc(full[tg], 1)

            def unit(u, m, par, kc, hi, lo, before=None, after=None):
                pe.wait_ge(w_lo_s, u + 1)
                mb_ = 8 // kc
                for b in range(mb_):
                    for tg in range(3):
                        if before and b == 0:
                            before(tg)
                        job(m + b, par, b, tg, kc, P * mb_, hi, lo)
                        if after:
                            after(b, tg)

            pe.sem_inc(at_s, 3)
            pe.sem_inc(at_t1, 2)
            pe.sem_inc(at_pv, 1)
            pe.sem_inc(at_ot, 2)
            pe.wait_ge(ident_s, 1)
            for t in range(9):
                src, rows = (xin[t], P) if t < 8 else (xins, NS)
                pe.wait_ge(x_h, t + 1)
                if t >= 1:
                    pe.wait_ge(x_lo, t)
                for k in range(KD):
                    ins = turn(psT[k // 4][:, P * (k % 4):P * (k % 4) + rows], src[0:rows, P * k:P * k + P])
                ins.then_inc(x_t, 1)
            pe.wait_ge(gains_in, 48)
            turn(psC[:, 0:24], gpack[:, :]).then_inc(gains_t, 1)
            pe.wait_ge(tril_s, 4)
            for g in range(4):
                ins = turn(psA[:, P * g:P * g + P], wsg[:, g, :])
            ins.then_inc(ws_t, 1)

            with pe.Fori(0, 4) as i:
                for j in range(2):
                    unit(2 * i + j, 2 * i + j, j, 8, h_hi, h_lo, before=lambda tg: pe.wait_ge(x_lo, TILES_OF[tg]))

            def kv_turns(pair):
                for tg in range(3):
                    pe.wait_ge(free[tg], M0[f"qkv{pair}"] + 10)
                n = 0
                tiles = []
                for g in range(GROUPS):
                    tiles += [vT[:, g, 512 * hh + r:512 * hh + 512:4] for hh in range(2) for r in range(4)]
                    if g == 0:
                        tiles.append(vT[:, 0, 384:512])
                lots = [tiles[4 * a:4 * a + 4] for a in range(7)]
                keys = [qk[:, 3 + g, 256 * r + 128:256 * r + 256] for g in range(2) for r in range(4)]
                keys += [qk[:, 5, 256 * r + 128 * hh:256 * r + 128 * hh + 128] for hh in range(2) for r in range(4)]
                lots += [keys[4 * a:4 * a + 4] for a in range(4)]
                for a, lot in enumerate(lots):
                    before = (6 if a % 2 == 0 else 5) * pair + a // 2
                    if before:
                        pe.wait_ge(kv_c[a % 2], before)
                    for b, src in enumerate(lot):
                        ins = turn(psT[a % 2][:, P * b:P * b + P], src)
                    ins.then_inc(kv_t, 1)

            def ln_turn(c):
                n = P if c < 8 else NS
                pe.wait_ge(ln_v, c + 1)
                for g in range(4):
                    ins = turn(psT[0][0:n, P * g:P * g + P], vc[:, g, 0:n])
                ins.then_inc(ln_t, 1)

            def ln_mixing(c):
                if c == 0:
                    pe.wait_ge(ws_c, 1)
                if c < 8:
                    pe.wait_ge(ln_n, c + 1)
                    if c:
                        pe.wait_ge(ln_o, c)
                    for g in range(4):
                        ins = mm(psA[:, P * g:P * g + P], vt[:, P * g:P * g + P], wsT[:, g, :], start=True, stop=True)
                else:
                    pe.wait_ge(ln_w, 1)
                    pe.wait_ge(ln_o, 8)
                    for g in range(4):
                        ins = turn(psA[:, P * g:P * g + NS], vw[:, P * g:P * g + P])
                ins.then_inc(ln_mix, 1)

            for j in range(9):
                u, m = U0["qkv0"] + j, M0["qkv0"] + j

                def after(b, tg, j=j):
                    if tg == 0:
                        ln_turn(j)
                    if tg == 2:
                        ln_mixing(j)
                unit(u, m, u % 2, 8, h_hi, h_lo, after=after)
            kv_turns(0)
            pe.wait_ge(ln_lo, 9)
            with pe.Fori(0, 2) as i:
                for j in range(2):
                    unit(U0["pb"] + 2 * i + j, M0["pb"] + 4 * i + 2 * j, (U0["pb"] + j) % 2, 4, ob_hi, ob_lo)

            def attention(pair, U, M):
                def scores(i, n):
                    r, hh, e = 2 * i + n // 4, n // 2 % 2, n % 2
                    N, T = 16 * pair + 8 * i + n, 8 * pair + 4 * i + n // 2
                    pe.wait_ge(at_q, 2 * T + 2)
                    pe.wait_ge(at_m, N + 1)
                    kr = qk[:, 3, 0:SEQ].rearrange("p (c i) -> p c i", c=4)
                    w = P * (hh + 1)
                    mm(psA[:, :].rearrange("p (c i) -> p c i", c=4), qst[:, hh, e, 0, :], kr[:, :, P * hh:P * hh + P],
                       start=True, stop=True)
                    if hh:
                        mm(psC[:, 0:P].rearrange("p (i c) -> p i c", c=4), qst[:, hh, e, 0, :],
                           kr.rearrange("p c i -> p i c")[:, 96:128, :], start=True, stop=True)
                    for g in (1, 2):
                        ins = mm(psB[:, w * (g - 1):w * g], qst[:, hh, e, g, :], qk[:, 3 + g, bass.ds(256 * r, w)],
                                 start=True, stop=True)
                    ins.then_inc(at_s, 1)

                def turns(i, n):
                    N, nb = 16 * pair + 8 * i + n, 9 if n // 2 % 2 else 6
                    pe.wait_ge(at_p, N + 1)
                    pe.wait_ge(at_c0, N + 1)
                    pe.wait_ge(at_c1, N + 1)
                    for b in range(nb):
                        if b == 8:
                            pe.wait_ge(at_o, N + 1)
                            pe.wait_ge(at_oc, 8 * pair + 4 * i + n // 2 + 1)
                        out = psO[:, 256:384] if b == 8 else psT[b // 4][:, P * (b % 4):P * (b % 4) + P]
                        ins = turn(out, pr[:, n % 2, P * b:P * b + P])
                        if b == 3:
                            ins.then_inc(at_t0, 1)
                    ins.then_inc(at_t1, 1)

                def pv(i, n):
                    r, hh, e = 2 * i + n // 4, n // 2 % 2, n % 2
                    N = 16 * pair + 8 * i + n
                    hd = slice(HD * e, HD * e + HD)
                    pe.wait_ge(at_c0, N + 2)
                    pe.wait_ge(at_c1, N + 2)
                    pe.wait_ge(at_o, N + 1)
                    pe.wait_ge(at_oc, 8 * pair + 4 * i + n // 2 + 1)
                    values = [vtok[:, 4 * hh + c, hd] for c in range(4)]
                    for g in (1, 2):
                        values += [vtok[:, 9 + 8 * (g - 1) + 4 * q + r, hd] for q in range(hh + 1)]
                    if hh:
                        values.append(vtok[:, 8, hd])
                    for b, v in enumerate(values):
                        ins = mm(psO[:, P:P + HD], prT[:, b, :], v, start=(b == 0), stop=(b == len(values) - 1))
                    ins.then_inc(at_pv, 1)

                def oturn(i, t):
                    T = 8 * pair + 4 * i + t
                    pe.wait_ge(at_o, 2 * T + 3)
                    pe.wait_ge(at_oc, T + 1)
                    turn(psO[:, 384:512], otok[:, t % 2, :]).then_inc(at_ot, 1)

                def gate(i, q):
                    par = (U + q // 3) % 2
                    if q % 3 == 0:
                        pe.wait_ge(w_lo_s, U + 2 * i + q // 3 + 1)
                    m = M + 2 * i + q // 3
                    pe.wait_ge(free[(q - 2) % 3], M + 2 * i + (q - 2) // 3 + 2)
                    job(m, par, 0, q % 3, 8, P, h_hi, h_lo, gbank[q % 2])

                pe.wait_ge(kv_c[0], 6 * (pair + 1))
                pe.wait_ge(kv_c[1], 5 * (pair + 1))
                pe.wait_ge(free[2], M + 1)
                with pe.Fori(0, 2) as i:
                    scores(i, 0)
                    gate(i, 0)
                    done = 1
                    for n in range(1, 9):
                        if n < 8:
                            scores(i, n)
                        if n in (3, 5, 7):
                            oturn(i, (n - 3) // 2)
                        turns(i, n - 1)
                        if n in (2, 3, 5, 6, 8):
                            gate(i, done)
                            done += 1
                        pv(i, n - 1)
                    oturn(i, 3)
                pe.wait_ge(at_oc, 8 * pair + 9)
                for tg in range(3):
                    pe.wait_ge(free[tg], M + 5)

            attention(0, U0["gb0"], M0["gb0"])
            for j in range(9):
                u = U0["qkv1"] + j
                unit(u, M0["qkv1"] + j, u % 2, 8, h_hi, h_lo)
            kv_turns(1)
            attention(1, U0["gb1"], M0["gb1"])

            def k_turn(kk):
                ck = CKEYS[kk % 3]
                pe.wait_ge(sk_in[kk % 4], 16 * (kk // 4 + 1))
                if kk >= 2:
                    pe.wait_ge(s_kc, kk - 1)
                for p in range(2):
                    ins = turn(psT[kk % 2][:, ck * p:ck * p + ck], kraw[0:ck, kk % 4, P * p:P * p + P])
                ins.then_inc(s_kt, 1)

            def k_scores(kk):
                n, g = kk // 3, kk % 3
                ck = CKEYS[g]
                pe.wait_ge(s_kc, kk + 1)
                if kk == 0:
                    pe.wait_ge(s_qz, 1)
                for p in range(2):
                    c = 32 * g + 4 * n + 2 * p
                    ins = mm(psA[0:ck, c:c + 2], kcT[:, kk % 2, ck * p:ck * p + ck], qz[:, p, g, n, :], start=True, stop=True)
                ins.then_inc(s_sc, 1)

            def sample_step(j, tg):
                if j == 0 and tg == 0:
                    for g in range(GROUPS):
                        for kv in range(2):
                            for p in range(2):
                                c = 256 * kv + P * p
                                ins = turn([psA, psB, psC][g][0:NS, c:c + P], sqkv[:, p, 3 + 3 * kv + g, :])
                    ins.then_inc(s_nt, 1)
                if j < 6:
                    if tg == 0:
                        k_turn(4 * j)
                        k_turn(4 * j + 1)
                    elif tg == 1:
                        if j == 0:
                            pe.wait_ge(s_nc, 3)
                        k_scores(4 * j)
                        k_scores(4 * j + 1)
                        k_turn(4 * j + 2)
                        k_turn(4 * j + 3)
                    else:
                        k_scores(4 * j + 2)
                        k_scores(4 * j + 3)
                elif j == 6 and tg == 0:
                    for g in range(GROUPS):
                        for p in range(2):
                            out = psB[0:NS, 32 * g:32 * g + 32].rearrange("k (n s) -> k n s", s=4)[:, :, 2 * p:2 * p + 2]
                            ins = mm(out, sqkv[:, p, 3 + g, :], qz[:, p, g], start=True, stop=True)
                    ins.then_inc(s_self, 1)
                elif j == 6 and tg == 1:
                    pe.wait_ge(s_sst, 3)
                    turn(psC[0:32, 0:128], sst[:, 0, 0:32])
                    turn(psC[0:32, 128:256], sst[:, 0, 32:64])
                    turn(psC[0:32, 256:288], sst[0:32, 0, 64:96])
                    for g in range(GROUPS):
                        ins = turn(psC[0:32, 288 + 8 * g:296 + 8 * g], sst[0:NS, 1, 32 * g:32 * g + 32])
                    ins.then_inc(s_rows, 1)
                elif j == 7 and tg == 0:
                    pe.wait_ge(s_pn, 1)
                    turn(psA[:, 0:32], ssr[:, 0:128])
                    turn(psA[:, 32:64], ssr[:, 128:256])
                    turn(psA[0:32, 64:96], ssr[:, 256:288])
                    for g in range(GROUPS):
                        ins = turn(psA[0:NS, 96 + 32 * g:128 + 32 * g], ssr[:, 288 + 8 * g:296 + 8 * g])
                    ins.then_inc(s_pt, 1)
                elif j == 7 and tg == 1:
                    pe.wait_ge(s_ptc, 3)
                    pe.wait_ge(sv_in, 16 * 24)
                    first = True
                    for g in range(GROUPS):
                        for p in range(2):
                            out = psB[:, 16 * p:16 * p + 16].rearrange("k (n e) -> k n e", e=2)
                            w = spT[0:NS, 3 + g, :].rearrange("k (n s) -> k n s", s=4)[:, :, 2 * p:2 * p + 2]
                            mm(out, svt[:, g, 1, P * p:P * p + P], w, start=first, stop=False, skip_group_check=True)
                            first = False
                    for kk in range(24):
                        n, g = kk // 3, kk % 3
                        ck = CKEYS[g]
                        for p in range(2):
                            ins = mm(psB[:, 16 * p + 2 * n:16 * p + 2 * n + 2], cv[0:ck, kk, P * p:P * p + P],
                                     spT[0:ck, g, 4 * n + 2 * p:4 * n + 2 * p + 2], start=False,
                                     stop=(kk == 23 and p == 1), skip_group_check=True)
                    ins.then_inc(s_pv, 1)

            for j in range(8):
                u = U0["ga"] + j
                unit(u, M0["ga"] + j, u % 2, 8, h_hi, h_lo, after=lambda b, tg, j=j: sample_step(j, tg))
            for j in range(2):
                u = U0["pa"] + j
                unit(u, M0["pa"] + 4 * j, u % 2, 2, oa_hi, oa_lo, before=lambda tg: pe.wait_ge(oa_s, tg + 1))

            def x_turn(t):
                rows = P if t < 8 else NS
                pe.wait_ge(xr_in[t % 2], 16 * (t // 2 + 1))
                if t:
                    pe.wait_ge(xr_c[0], t)
                    pe.wait_ge(xr_c[1], t)
                for k in range(KD):
                    ins = turn(psT[k // 4][:, P * (k % 4):P * (k % 4) + rows], xre[0:rows, t % 2, P * k:P * k + P])
                ins.then_inc(xr_t, 1)

            for j in range(8):
                u = U0["wo"] + j

                def after(b, tg, j=j):
                    if tg == 0:
                        x_turn(j)
                    if tg == 1 and j == 7:
                        x_turn(8)
                unit(u, M0["wo"] + j, u % 2, 8, m_hi, m_lo, after=after,
                     before=(lambda tg: pe.wait_ge(m_l, 21 + tg + 1)) if j == 0 else None)

            def norm(phase, tg):
                s, done = ((y1_a, 21 + tg + 1), (x1_a, 8 * (tg + 1)), (y2_a, 21 + tg + 1))[phase]
                q = 3 * phase + tg
                pe.wait_ge(s, done)
                if q:
                    pe.wait_ge(n_v, q)
                for j in range(3):
                    ins = mm(psC[:, j:j + 1], acc[:, tg, NOFF[j]:NOFF[j] + P], ones[:, 0:1], start=True, stop=True)
                ins.then_inc(n_s, 1)
                pe.wait_ge(n_d, q + 1)
                if q >= 2:
                    pe.wait_ge((x1_t, f_t, z_t)[(q - 2) // 3], 8 * ((q - 2) % 3 + 1))
                for j in range(3):
                    ins = mm(psR[q % 2][:, NOFF[j]:NOFF[j] + P], ones[:, :], diag[:, j, :], start=True, stop=True)
                ins.then_inc(n_b, 1)

            for what, phase, tg in NORMS:
                if what == "chain":
                    norm(phase, tg)

            f_ready = lambda tg: pe.wait_ge(f_l, 8 * (tg + 1))
            with pe.Fori(0, ROUNDS) as i:
                for j in range(2 * FG):
                    unit(U0["ffn"] + 12 * i + j, M0["ffn"] + 16 * i + j, j % 2, 8, f_hi, f_lo,
                         before=f_ready if j == 0 else None)
                for j in range(4):
                    unit(U0["ffn"] + 12 * i + 8 + j, M0["ffn"] + 16 * i + 8 + 2 * j, j % 2, 4, a_hi, a_lo,
                         before=(lambda tg: pe.wait_ge(ff_l, 12 * i + 9 + tg + 3)) if j == 0 else None)
            for j in range(4):
                unit(U0["tail"] + j, M0["tail"] + j, j % 2, 8, f_hi, f_lo)
            for j in range(2):
                unit(U0["tail"] + 4 + j, M0["tail"] + 4 + 4 * j, j % 2, 2, a_hi, a_lo,
                     before=(lambda tg: pe.wait_ge(ff_l, 12 * ROUNDS + 3 + tg + 3)) if j == 0 else None)
            for tg in range(3):
                norm(2, tg)
            for t in range(9):
                rows = P if t < 8 else NS
                pe.wait_ge(z_s, 8 * (1 if t < 2 else 2 if t < 5 else 3))
                if t:
                    pe.wait_ge(z_c[0], t)
                    pe.wait_ge(z_c[1], t)
                for k in range(KD):
                    ins = turn(psT[k // 4][0:rows, P * (k % 4):P * (k % 4) + P], xT[:, k, P * t:P * t + rows])
                ins.then_inc(z_turn, 1)

        def by4(ps, n=P):
            return ps[:, :].rearrange("p (k n) -> p k n", k=4)[:, :, 0:n]

        @block.scalar
        def _(act):
            fn = nc.scalar.activation
            act.sem_inc(at_c0, 1)
            act.sem_inc(at_oc, 1)

            def split(u, par, m_used):
                act.wait_ge(w_in_s[par], 16 * (u // 2 + 1) if isinstance(u, int) else u)
                if m_used is not None:
                    act.wait_ge(full[2], m_used)
                fn(w_hi[par][:], w_raw[par][:], ACT.Copy).then_inc(w_hi_s, 1)

            def split_in(u0, per, i, j, m_used):
                u = u0 + j + 2
                par = u % 2
                if isinstance(i, int):
                    u += per * i
                    if u < UNITS:
                        split(u, par, m_used)
                    return
                act.wait_ge(w_in_s[par], 16 * (u // 2 + 1) + 8 * per * i)
                act.wait_ge(full[2], m_used)
                fn(w_hi[par][:], w_raw[par][:], ACT.Copy).then_inc(w_hi_s, 1)

            def square(t):
                src, rows = (xin[t], P) if t < 8 else (xins, NS)
                act.wait_ge(x_in[t], 16)
                if t == 8:
                    act.wait_ge(x_sq, 1)
                fn(uv[0:rows, t % 8, 0:D], src[0:rows, :], ACT.Square, accum_out=stat[0:rows, t:t + 1]).then_inc(x_sq, 1)

            def x_high(t):
                n = P if t < 8 else NS
                act.wait_ge(x_t, t + 1)
                for a in range(2):
                    fn(h_hi[:, 4 * a:4 * a + 4, P * t:P * t + n], by4(psT[a], n), ACT.Copy).then_inc(x_hi, 1)

            square(0)
            for t in range(9):
                if t < 8:
                    square(t + 1)
                rows = P if t < 8 else NS
                act.wait_ge(x_v, t + 1)
                fn(stat[0:rows, 18 + t:19 + t], stat[0:rows, 9 + t:10 + t], ACT.Sqrt).then_inc(x_sd, 1)
                if t:
                    x_high(t - 1)
            split(0, 0, None)
            x_high(8)
            split(1, 1, None)
            act.wait_ge(gains_t, 1)
            fn(gains[:, :, :].rearrange("p a k -> p (a k)"), psC[:, 0:24], ACT.Copy).then_inc(gains_s, 1)
            act.wait_ge(ws_t, 1)
            fn(wsT[:, :, :].rearrange("p g t -> p (g t)"), psA[:, :], ACT.Copy).then_inc(ws_c, 1)

            with act.Fori(0, 4) as i:
                for j in range(2):
                    for tg in range(3):
                        act.wait_ge(full[tg], 2 * i + j + 1)
                        fn(uv[:, 2 * i + j, tgc[tg]], bank[tg][:, 0:TG], ACT.Copy).then_inc(free[tg], 1)
                    split_in(0, 2, i, j, 2 * i + j + 1)

            def qkv_copy(pair, j, tg):
                act.wait_ge(full[tg], M0[f"qkv{pair}"] + j + 1)
                src = bank[tg][:, 0:TG]
                n = TG // 4 if tg < 2 else (SEQ - 2 * TG) // 4
                last = []
                if j < 6:
                    out = qk[:, j, 0:SEQ].rearrange("p (r i) -> p r i", r=4)[:, :, TG // 4 * tg:TG // 4 * tg + n]
                    a = fn(out, src[:, 0:4 * n].rearrange("p (i r) -> p r i", r=4), ACT.Copy)
                else:
                    a = fn(vT[:, j - 6, TG * tg:TG * tg + 4 * n], src[:, 0:4 * n], ACT.Copy)
                if tg == 2:
                    a.then_inc(act_s, 1)
                    a = fn(sqkv[:, pair, j, :], src[:, 4 * n:TG], ACT.Copy)
                    act.wait_ge(act_s, 9 * pair + j + 1)
                a.then_inc(free[tg], 1)

            def kv_copy(pair):
                for a in range(0, 11, 2):
                    act.wait_ge(kv_t, 11 * pair + a + 1)
                    n = 1 if a == 6 else 4
                    out = vtok[:, 4 * a:4 * a + n] if a < 7 else kst[:, 4 * (a - 7):4 * (a - 7) + 4]
                    fn(out, by4(psT[0])[:, 0:n], ACT.Copy).then_inc(kv_c[0], 1)

            def gelus(c):
                n = P if c < 8 else NS
                cols = slice(P * c, P * c + n)
                if c:
                    act.wait_ge(ln_t, c)
                fn(vc[:, :, 0:n], uv[:, 4:8, cols], ACT.Gelu_apprx_tanh).then_inc(ln_v, 1)
                fn(uv[:, 0:4, cols], uv[:, 0:4, cols], ACT.Gelu_apprx_tanh).then_inc(ln_u, 1)

            for tg in range(3):
                act.wait_ge(free[tg], M0["qkv0"] + 1)
            gelus(0)
            for j in range(9):
                n = P if j < 8 else NS
                rows = n
                qkv_copy(0, j, 0)
                act.wait_ge(ln_var, j + 1)
                fn(stat[0:rows, 40:41], stat[0:rows, 39:40], ACT.Sqrt).then_inc(ln_sd, 1)
                qkv_copy(0, j, 1)
                qkv_copy(0, j, 2)
                act.wait_ge(ln_o, j + 1)
                fn(ob_hi[:, :, P * j:P * j + n], mixt[:, :, 0:n], ACT.Copy).then_inc(ln_hi, 1)
                if j < 8:
                    gelus(j + 1)
                split_in(U0["qkv0"], 0, 0, j, M0["qkv0"] + j + 1)
            kv_copy(0)

            act.wait_ge(sgv_out, 16)
            with act.Fori(0, 2) as i:
                for j in range(2):
                    for b in range(2):
                        for tg in range(3):
                            m = 4 * i + 2 * j + b
                            act.wait_ge(full[tg], M0["pb"] + m + 1)
                            fn(mb[:, m, tgc[tg]], bank[tg][:, 0:TG], ACT.Copy, scale=0.5).then_inc(free[tg], 1)
                    split_in(U0["pb"], 2, i, j, M0["pb"] + 4 * i + 2 * j + 2)

            def attention(pair, U, M):
                def probs(i, n):
                    N, w = 16 * pair + 8 * i + n, 1152 if n // 2 % 2 else 768
                    act.wait_ge(at_m, N + 2)
                    fn(pr[:, n % 2, 0:w], pr[:, n % 2, 0:w], ACT.Exp, scale=SCALE, bias=stat[:, 48 + n % 2:49 + n % 2],
                       accum_out=stat[:, 50 + n % 2:51 + n % 2]).then_inc(at_p, 1)

                def copy0(i, n):
                    N = 16 * pair + 8 * i + n
                    act.wait_ge(at_t0, N + 1)
                    act.wait_ge(at_pv, N + 1)
                    fn(prT[:, 0:4, :], by4(psT[0]), ACT.Copy).then_inc(at_c0, 1)

                def ocopy(i, t):
                    T = 8 * pair + 4 * i + t
                    act.wait_ge(at_ot, T + 3)
                    out = oaT[:, pair, 0:SEQ].rearrange("p (h i r) -> p h r i", h=2, r=4)
                    fn(out[:, t % 2, bass.ds(2 * i + t // 2, 1), :].rearrange("p o i -> p (o i)"), psO[:, 384:512],
                       ACT.Copy).then_inc(at_oc, 1)

                def gate(i, q):
                    m, G = M + 2 * i + q // 3, 12 * pair + 6 * i + q
                    act.wait_ge(full[q % 3], m + 1)
                    act.wait_ge(at_gu, G + 1)
                    fn(gt[:, q % 2, :], gbank[q % 2][:, 0:TG], ACT.Tanh, scale=0.5).then_inc(free[q % 3], 1)
                    if q % 3 == 2:
                        split_in(U, 2, i, q // 3, m + 1)

                with act.Fori(0, 2) as i:
                    probs(i, 0)
                    gate(i, 0)
                    done = 1
                    for n in range(1, 9):
                        if n in (3, 5, 7):
                            ocopy(i, (n - 3) // 2)
                        copy0(i, n - 1)
                        if n < 8:
                            probs(i, n)
                        if n in (2, 3, 5, 6, 8):
                            gate(i, done)
                            done += 1
                    ocopy(i, 3)

            attention(0, U0["gb0"], M0["gb0"])
            for j in range(9):
                if j == 6:
                    act.wait_ge(kv_d, 16 * 32)
                for tg in range(3):
                    qkv_copy(1, j, tg)
                split_in(U0["qkv1"], 0, 0, j, M0["qkv1"] + j + 1)
            kv_copy(1)
            attention(1, U0["gb1"], M0["gb1"])

            act.wait_ge(kv_d, 16 * 64)
            for j in range(8):
                for tg in range(3):
                    act.wait_ge(full[tg], M0["ga"] + j + 1)
                    fn(ga[:, j, tgc[tg]], bank[tg][:, 0:TG], ACT.Tanh, scale=0.5).then_inc(free[tg], 1)
                    if j == 6 and tg == 1:
                        act.wait_ge(s_ssr, 1)
                        fn(ssr[:, 0:312], ssr[:, 0:312], ACT.Exp, scale=SCALE, bias=stat[0:32, 53:54],
                           accum_out=stat[0:32, 54:55]).then_inc(s_exp, 1)
                split_in(U0["ga"], 0, 0, j, M0["ga"] + j + 1)

            act.wait_ge(s_oa, 2)
            act.wait_ge(full[2], M0["pa"])
            for tg in range(3):
                fn(oa_hi[:, :, tgc[tg]], oaT[:, :, tgc[tg]], ACT.Copy).then_inc(oa_h, 1)
            for k in range(24):
                act.wait_ge(m_t, k + 1)
                fn(m_hi[:, k // 3, tgc[k % 3]], pt[:, 2 * (k % 2) + 1, :], ACT.Copy).then_inc(m_h, 1)
                if k % 12 == 11:
                    split_in(U0["pa"], 0, 0, k // 12, M0["pa"] + 4 * (k // 12) + 4)

            def x_copy(t):
                n = P if t < 8 else NS
                act.wait_ge(xr_t, t + 1)
                fn(xT[:, 0:4, P * t:P * t + n], by4(psT[0], n), ACT.Copy).then_inc(xr_c[0], 1)

            for j in range(8):
                for tg in range(3):
                    act.wait_ge(full[tg], M0["wo"] + j + 1)
                    fn(y1[:, j, tgc[tg]], bank[tg][:, 0:TG], ACT.Copy).then_inc(free[tg], 1)
                    if tg == 0:
                        x_copy(j)
                    if j == 7 and tg == 1:
                        x_copy(8)
                split_in(U0["wo"], 0, 0, j, M0["wo"] + j + 1)

            def root(phase, tg):
                act.wait_ge(n_v, 3 * phase + tg + 1)
                fn(stat[:, 3:6], stat[:, 0:3], ACT.Sqrt).then_inc(n_sd, 1)

            for what, phase, tg in NORMS:
                if what == "chain":
                    root(phase, tg)
                    continue
                for m in range(KD):
                    k = 8 * tg + m
                    if phase == 0:
                        act.wait_ge(x1_s, k + 1)
                        if k >= 2:
                            act.wait_ge(x1_a, k - 1)
                        fn(sq[:, k % 2, :], xT[:, m, tgc[tg]], ACT.Square).then_inc(x1_q, 1)
                    else:
                        act.wait_ge(f_t, k + 1)
                        fn(f_hi[:, m, tgc[tg]], nt_[:, (24 + k) % 3, :], ACT.Copy).then_inc(f_h, 1)

            def silu(m, tg):
                act.wait_ge(full[tg], m + 1)
                fn(sg[:, tgc[tg]], bank[tg][:, 0:TG], ACT.Silu).then_inc(free[tg], 1)

            def a_high(m, j, tg):
                act.wait_ge(free[tg], m + 2)
                fn(a_hi[:, j, tgc[tg]], sq[:, (3 * j + tg) % 2, :], ACT.Copy).then_inc(ff_h, 1)

            with act.Fori(0, ROUNDS) as i:
                for j in range(FG):
                    m = M0["ffn"] + 16 * i + 2 * j
                    for tg in range(3):
                        silu(m, tg)
                    split_in(U0["ffn"], 12, i, 2 * j, m + 1)
                    for tg in range(3):
                        a_high(m + 1, j, tg)
                    split_in(U0["ffn"], 12, i, 2 * j + 1, m + 2)
                for j in range(4):
                    split_in(U0["ffn"], 12, i, 8 + j, M0["ffn"] + 16 * i + 8 + 2 * j + 2)
            for j in range(2):
                m = M0["tail"] + 2 * j
                for tg in range(3):
                    silu(m, tg)
                split_in(U0["tail"], 0, 0, 2 * j, m + 1)
                for tg in range(3):
                    a_high(m + 1, j, tg)
                split_in(U0["tail"], 0, 0, 2 * j + 1, m + 2)
            act.wait_ge(ff_l, 3 * KF + 2)
            for k in range(24):
                act.wait_ge(free[k % 3], M0["tail"] + 4 + k // 3 + 2)
                if k >= 2:
                    act.wait_ge(y2_a, k - 1)
                fn(sq[:, k % 2, :], y2[:, k // 3, tgc[k % 3]], ACT.Square).then_inc(y2_q, 1)
            for tg in range(3):
                root(2, tg)
            for t in range(9):
                rows = P if t < 8 else NS
                act.wait_ge(z_turn, t + 1)
                if t >= 2:
                    act.wait_ge(z_out[t % 2], 16 * (t // 2))
                fn(yt[0:rows, t % 2, 0:512], psT[0][0:rows, :], ACT.Copy).then_inc(z_c[0], 1)

        @block.vector
        def _(dve):
            v = nc.vector
            st = Steps(dve, dve_s)
            for tg in range(3):
                dve.sem_inc(free[tg], 1)
            dve.sem_inc(at_m, 1)
            dve.sem_inc(at_c1, 1)
            dve.sem_inc(at_o, 1)
            dve.sem_inc(at_gu, 2)

            def lo_split(u, par):
                dve.wait_ge(w_hi_s, u + 1)
                v.tensor_tensor(w_lo[par][:], w_raw[par][:], w_hi[par][:].bitcast(F32), ALU.subtract).then_inc(w_lo_s, 1)

            def lo_in(u0, per, i, j):
                par = (u0 + j) % 2
                u = u0 + j + 2 + per * i
                if not isinstance(u, int) or u < UNITS:
                    lo_split(u, par)

            def x_low(t):
                n = P if t < 8 else NS
                for a in range(2):
                    dve.wait_ge(x_hi, 2 * t + a + 1)
                    hi = h_hi[:, 4 * a:4 * a + 4, P * t:P * t + n].bitcast(F32)
                    ins = v.tensor_tensor(h_lo[:, 4 * a:4 * a + 4, P * t:P * t + n], by4(psT[a], n), hi, ALU.subtract)
                    if a == 0:
                        st.link(ins)
                ins.then_inc(x_lo, 1)

            for t in range(9):
                src, rows = (xin[t], P) if t < 8 else (xins, NS)
                dve.wait_ge(x_sq, t + 1)
                v.tensor_scalar(stat[0:rows, 9 + t:10 + t], stat[0:rows, t:t + 1], 1.0 / D, EPS, ALU.mult, ALU.add
                                ).then_inc(x_v, 1)
                dve.wait_ge(x_sd, t + 1)
                st.link(v.reciprocal(stat[0:rows, 27 + t:28 + t], stat[0:rows, 18 + t:19 + t]))
                dve.wait_ge(x_g, t + 1)
                v.tensor_scalar(src[0:rows, :], src[0:rows, :], stat[0:rows, 27 + t:28 + t], None, ALU.mult).then_inc(x_h, 1)
                if t:
                    x_low(t - 1)
            lo_split(0, 0)
            x_low(8)
            lo_split(1, 1)
            dve.wait_ge(iota_s, 1)
            st.link(v.tensor_single_scalar(iom[:], iot[:], 3, ALU.bitwise_and))
            v.tensor_scalar(m_far[:, 1, :], iom[:], 0.0, NEG, ALU.is_gt, ALU.mult).then_inc(far_s, 1)

            with dve.Fori(0, 4) as i:
                for j in range(2):
                    lo_in(0, 2, i, j)

            def kv_copy(pair):
                if pair:
                    dve.wait_ge(kv_d, 16 * 32)
                for a in range(1, 11, 2):
                    dve.wait_ge(kv_t, 11 * pair + a + 1)
                    out = vtok[:, 4 * a:4 * a + 4] if a < 7 else kst[:, 4 * (a - 7):4 * (a - 7) + 4]
                    v.tensor_copy(out, by4(psT[1])).then_inc(kv_c[1], 1)

            dve.wait_ge(small_in, 96)
            for c in range(9):
                n = P if c < 8 else NS
                dve.wait_ge(ln_t, c + 1)
                st.link(v.bn_stats(stat[0:n, 30:36], psT[0][0:n, :]))
                st.link(v.bn_aggr(stat[0:n, 36:38], stat[0:n, 30:36]))
                v.tensor_scalar(stat[0:n, 39:40], stat[0:n, 37:38], EPS, None, ALU.add).then_inc(ln_var, 1)
                dve.wait_ge(ln_sd, c + 1)
                st.link(v.reciprocal(stat[0:n, 41:42], stat[0:n, 40:41]))
                if c:
                    dve.wait_ge(ln_mix, c)
                st.link(v.tensor_scalar(vt[0:n, :], psT[0][0:n, :], stat[0:n, 36:37], stat[0:n, 41:42], ALU.subtract, ALU.mult))
                st.link(v.tensor_tensor(vt[0:n, :], vt[0:n, :], lnvg[0:n, :], ALU.mult))
                v.tensor_tensor(vt[0:n, :], vt[0:n, :], lnvb[0:n, :], ALU.add).then_inc(ln_n, 1)
                dve.wait_ge(ln_n, c + 1)
                if c == 8:
                    for g in range(4):
                        st.link(v.tensor_scalar(vw[:, P * g:P * g + P], vt[0:NS, P * g:P * g + P], w00[:, g:g + 1],
                                                w00[:, 4 + g:5 + g], ALU.mult, ALU.add))
                    dve.sem_inc(ln_w, 1)
                dve.wait_ge(ln_mix, c + 1)
                dve.wait_ge(ln_u, c + 1)
                cols = slice(P * c, P * c + n)
                if c < 8:
                    st.link(v.tensor_tensor(mixt[:], by4(psA), bsg[:], ALU.add))
                    v.tensor_tensor(mixt[:], mixt[:], uv[:, 0:4, cols], ALU.mult).then_inc(ln_o, 1)
                else:
                    v.tensor_tensor(mixt[:, :, 0:n], by4(psA, n), uv[:, 0:4, cols], ALU.mult).then_inc(ln_o, 1)
                dve.wait_ge(ln_hi, c + 1)
                v.tensor_tensor(ob_lo[:, :, cols], mixt[:, :, 0:n], ob_hi[:, :, cols].bitcast(F32), ALU.subtract
                                ).then_inc(ln_lo, 1)
                dve.wait_ge(ln_lo, c + 1)
                lo_in(U0["qkv0"], 0, 0, c)
            kv_copy(0)
            with dve.Fori(0, 2) as i:
                for j in range(2):
                    lo_in(U0["pb"], 2, i, j)

            dve.wait_ge(masks_s, 1)

            def attention(pair, U, M):
                def maxima(i, n):
                    r, hh = 2 * i + n // 4, n // 2 % 2
                    N, s_ = 16 * pair + 8 * i + n, n % 2
                    mx = [stat[:, 42 + 3 * s_ + a:43 + 3 * s_ + a] for a in range(3)]
                    w = P * (hh + 1)
                    dve.wait_ge(at_s, N + 4)
                    dve.wait_ge(at_t1, N + 1)
                    if n % 4 == 0:
                        st.link(v.tensor_copy(m_now[:], m_main[:, bass.ds(3 - r, 4), :]))
                        st.link(v.tensor_copy(e_now[:], m_edge[:, :, bass.ds(3 - r, 4)]))

                    v.memset(stat[:, 63:64], 0.0)

                    def add_max(out, in0, in1, accum):
                        return v.tensor_tensor_reduce(out, in0, in1, 1.0, NEG, ALU.add, ALU.max, accum)

                    far = add_max(pr[:, s_, 512:512 + 2 * w].rearrange("p (g i) -> p g i", g=2),
                                  psB[:, 0:2 * w].rearrange("p (g i) -> p g i", g=2), m_far[:, :, 256 - w:256], mx[1])
                    st.mark(far)
                    if hh:
                        st.mark(add_max(pr[:, s_, 1024:1152].rearrange("p (i c) -> p i c", c=4),
                                        psC[:, 0:P].rearrange("p (i c) -> p i c", c=4), e_now[:], mx[2]))
                    st.link(add_max(pr[:, s_, 0:512].rearrange("p (c i) -> p c i", c=4),
                                    psA[:, :].rearrange("p (c i) -> p c i", c=4), m_now[:], mx[0]))
                    if hh:
                        st.link(v.tensor_scalar(mx[0], mx[0], mx[2], None, ALU.max))
                    v.tensor_scalar(stat[:, 48 + s_:49 + s_], mx[0], mx[1], -SCALE, ALU.max, ALU.mult).then_inc(at_m, 1)

                def copy1(i, n):
                    N, hh = 16 * pair + 8 * i + n, n // 2 % 2
                    dve.wait_ge(at_t1, N + 3)
                    dve.wait_ge(at_pv, N + 1)
                    ins = v.tensor_copy(prT[:, 4:8 if hh else 6, :], by4(psT[1])[:, 0:4 if hh else 2])
                    if hh:
                        st.link(ins)
                        ins = v.tensor_copy(prT[:, 8, :], psO[:, 256:384])
                    ins.then_inc(at_c1, 1)

                def gated(i, q):
                    G = 12 * pair + 6 * i + q
                    part = mb[:, bass.ds(4 * pair + 2 * i + q // 3, 1), tgc[q % 3]].rearrange("p o t -> p (o t)")
                    dve.wait_ge(free[q % 3], M + 2 * i + q // 3 + 2)
                    v.scalar_tensor_tensor(part, gt[:, q % 2, :], 1.0, part, ALU.add, ALU.mult).then_inc(at_gu, 1)
                    if q % 3 == 2:
                        lo_in(U, 2, i, q // 3)

                def outputs(i, n):
                    N, T = 16 * pair + 8 * i + n, 8 * pair + 4 * i + n // 2
                    e = n % 2
                    dve.wait_ge(at_pv, N + 2)
                    dve.wait_ge(at_ot, T + 1)
                    st.link(v.reciprocal(stat[:, 52:53], stat[:, 50 + e:51 + e]))
                    v.tensor_scalar(otok[:, n // 2 % 2, HD * e:HD * e + HD], psO[:, P:P + HD], stat[:, 52:53], None, ALU.mult
                                    ).then_inc(at_o, 1)

                with dve.Fori(0, 2) as i:
                    st.enter(i, 4 * 2 + 4 * 4 + 4 + 4 + 8)
                    maxima(i, 0)
                    gated(i, 0)
                    done = 1
                    for n in range(1, 9):
                        copy1(i, n - 1)
                        if n < 8:
                            maxima(i, n)
                        if n in (2, 3, 5, 6, 8):
                            gated(i, done)
                            done += 1
                        outputs(i, n - 1)
                st.leave(2)

            attention(0, U0["gb0"], M0["gb0"])
            for j in range(9):
                lo_in(U0["qkv1"], 0, 0, j)
            kv_copy(1)
            attention(1, U0["gb1"], M0["gb1"])

            dve.wait_ge(kv_d, 16 * 64)
            dve.wait_ge(at_oc, 17)
            st.link(v.memset(qz[:], 0.0))
            for p in range(2):
                for e in range(2):
                    hd = slice(HD * e, HD * e + HD)
                    st.link(v.tensor_copy(qz[hd, p, :, :, e], sqkv[hd, p, 0:3, :]))
            dve.sem_inc(s_qz, 1)
            dve.wait_ge(s_nt, 1)
            for g in range(GROUPS):
                v.tensor_copy(svt[:, g].rearrange("b k c -> b (k c)"), [psA, psB, psC][g][0:NS, :]).then_inc(s_nc, 1)

            def k_copy(kk):
                ck = CKEYS[kk % 3]
                dve.wait_ge(s_kt, kk + 1)
                if kk >= 2:
                    dve.wait_ge(s_sc, kk - 1)
                v.tensor_copy(kcT[:, kk % 2, 0:2 * ck], psT[kk % 2][:, 0:2 * ck]).then_inc(s_kc, 1)

            for j in range(8):
                if j < 6:
                    for kk in range(4 * j, 4 * j + 4):
                        k_copy(kk)
                if j == 6:
                    dve.wait_ge(s_sc, 24)
                    dve.wait_ge(s_self, 1)
                    v.tensor_copy(sst[:, 0, 0:64], psA[:, 0:64]).then_inc(s_sst, 1)
                    v.tensor_copy(sst[0:32, 0, 64:96], psA[0:32, 64:96]).then_inc(s_sst, 1)
                    v.tensor_copy(sst[0:NS, 1, :], psB[0:NS, 0:96]).then_inc(s_sst, 1)
                    dve.wait_ge(s_rows, 1)
                    dve.wait_ge(masks_s, 2)
                    st.link(v.tensor_copy(ssr[:, 0:288], psC[0:32, 0:288]))
                    st.link(v.tensor_tensor(ssr[:, 288:312], psC[0:32, 288:312], smask[:].rearrange("p g n -> p (g n)"), ALU.add))
                    st.link(v.reduce_max(stat[0:32, 55:56], ssr[:, 0:312], mybir.AxisListType.X))
                    v.tensor_scalar(stat[0:32, 53:54], stat[0:32, 55:56], -SCALE, None, ALU.mult).then_inc(s_ssr, 1)
                    dve.wait_ge(s_exp, 1)
                    st.link(v.reciprocal(stat[0:32, 56:57], stat[0:32, 54:55]))
                    v.tensor_scalar(ssr[:, 0:312], ssr[:, 0:312], stat[0:32, 56:57], None, ALU.mult).then_inc(s_pn, 1)
                if j == 7:
                    dve.wait_ge(s_pt, 1)
                    v.tensor_copy(spT[:, 0:2, :].rearrange("p g n -> p (g n)"), psA[:, 0:64]).then_inc(s_ptc, 1)
                    v.tensor_copy(spT[0:32, 2, :], psA[0:32, 64:96]).then_inc(s_ptc, 1)
                    v.tensor_copy(spT[0:NS, 3:6, :].rearrange("p g n -> p (g n)"), psA[0:NS, 96:192]).then_inc(s_ptc, 1)
                lo_in(U0["ga"], 0, 0, j)
            dve.wait_ge(s_pv, 1)
            for e in range(2):
                hd = slice(HD * e, HD * e + HD)
                v.tensor_copy(oaT[hd, :, SEQ:NT], psB[hd, 0:32].rearrange("d (p n e) -> d p n e", p=2, e=2)[:, :, :, e]
                              ).then_inc(s_oa, 1)

            for tg in range(3):
                dve.wait_ge(oa_h, tg + 1)
                v.tensor_tensor(oa_lo[:, :, tgc[tg]], oaT[:, :, tgc[tg]], oa_hi[:, :, tgc[tg]].bitcast(F32), ALU.subtract
                                ).then_inc(oa_s, 1)
            for k in range(24):
                m, tg = k // 3, k % 3
                a, b = pt[:, 2 * (k % 2), :], pt[:, 2 * (k % 2) + 1, :]
                dve.wait_ge(full[tg], M0["pa"] + m + 1)
                if k >= 2:
                    dve.wait_ge(m_l, k - 1)
                v.scalar_tensor_tensor(a, ga[:, m, tgc[tg]], 1.0, bank[tg][:, 0:TG], ALU.add, ALU.mult).then_inc(free[tg], 1)
                dve.wait_ge(free[tg], M0["pa"] + m + 2)
                v.scalar_tensor_tensor(b, a, 0.5, mb[:, m, tgc[tg]], ALU.mult, ALU.add).then_inc(m_t, 1)
                if k % 12 == 11:
                    lo_in(U0["pa"], 0, 0, k // 12)

            def x_copy(t):
                n = P if t < 8 else NS
                dve.wait_ge(xr_t, t + 1)
                v.tensor_copy(xT[:, 4:8, P * t:P * t + n], by4(psT[1], n)).then_inc(xr_c[1], 1)

            for j in range(8):
                x_copy(j)
                if j == 7:
                    x_copy(8)
                lo_in(U0["wo"], 0, 0, j)

            def chain(phase, tg):
                q = 3 * phase + tg
                dve.wait_ge(n_s, q + 1)
                v.tensor_scalar(stat[:, 0:3], psC[:, 0:3], 1.0 / D, EPS, ALU.mult, ALU.add).then_inc(n_v, 1)
                dve.wait_ge(n_sd, q + 1)
                st.link(v.reciprocal(stat[:, 6:9], stat[:, 3:6]))
                if q:
                    dve.wait_ge(n_b, q)
                for j in range(3):
                    ins = v.tensor_scalar(diag[:, j, :], ident[:], stat[:, 6 + j:7 + j], None, ALU.mult)
                    if j < 2:
                        st.link(ins)
                ins.then_inc(n_d, 1)

            dve.wait_ge(gains_s, 1)
            dve.wait_ge(xr_t, 9)

            def slot_free(k):
                if 3 <= k < 27:
                    dve.wait_ge(x1_s, k - 2)
                elif k >= 27:
                    dve.wait_ge(f_l, k - 26)

            for what, phase, tg in NORMS:
                if what == "chain":
                    chain(phase, tg)
                    continue
                q = 3 * phase + tg
                dve.wait_ge(n_b, q + 1)
                for m in range(KD + 2):
                    k = 8 * tg + m
                    if m < KD:
                        kk = 24 * phase + k
                        slot_free(kk)
                        src = (y1 if phase == 0 else xT)[:, m, tgc[tg]]
                        v.scalar_tensor_tensor(nt_[:, kk % 3, :], src, gains[:, phase, m:m + 1], psR[q % 2][:, 0:TG],
                                               ALU.mult, ALU.mult).then_inc(x1_t if phase == 0 else f_t, 1)
                    if phase == 0 and m >= 2:
                        k -= 2
                        dve.wait_ge(x1_q, k + 1)
                        if m == 2:
                            v.tensor_copy(acc[:, tg, :], sq[:, k % 2, :]).then_inc(x1_a, 1)
                        else:
                            dve.wait_ge(x1_a, k)
                            v.tensor_tensor(acc[:, tg, :], acc[:, tg, :], sq[:, k % 2, :], ALU.add).then_inc(x1_a, 1)

            def product(m, j, tg, g3):
                dve.wait_ge(full[tg], m + 1)
                dve.wait_ge(ff_l, g3 + 1)
                v.tensor_tensor(sq[:, (3 * j + tg) % 2, :], bank[tg][:, 0:TG], sg[:, tgc[tg]], ALU.mult).then_inc(free[tg], 1)

            def y2_add(m, c, tg):
                dve.wait_ge(full[tg], m + 1)
                part = y2[:, c, tgc[tg]]
                v.tensor_tensor(part, part, bank[tg][:, 0:TG], ALU.add).then_inc(free[tg], 1)

            with dve.Fori(0, ROUNDS) as i:
                for j in range(FG):
                    lo_in(U0["ffn"], 12, i, 2 * j)
                    for tg in range(3):
                        product(M0["ffn"] + 16 * i + 2 * j + 1, j, tg, 12 * i + 3 * j + tg)
                    lo_in(U0["ffn"], 12, i, 2 * j + 1)
                dve.wait_ge(y2_z, 1)
                for j in range(4):
                    for b in range(2):
                        for tg in range(3):
                            y2_add(M0["ffn"] + 16 * i + 8 + 2 * j + b, 2 * j + b, tg)
                    lo_in(U0["ffn"], 12, i, 8 + j)
            for j in range(2):
                lo_in(U0["tail"], 0, 0, 2 * j)
                for tg in range(3):
                    product(M0["tail"] + 2 * j + 1, j, tg, 12 * ROUNDS + 3 * j + tg)
                lo_in(U0["tail"], 0, 0, 2 * j + 1)
            for k in range(24):
                y2_add(M0["tail"] + 4 + k // 3, k // 3, k % 3)
            for what, phase, tg in LAST_NORM:
                if what == "chain":
                    chain(phase, tg)
                    continue
                q = 3 * phase + tg
                dve.wait_ge(n_b, q + 1)
                for m in range(KD):
                    k = 8 * tg + m
                    if k >= 3:
                        dve.wait_ge(z_s, k - 2)
                    v.scalar_tensor_tensor(nt_[:, k % 3, :], y2[:, m, tgc[tg]], gains[:, 2, m:m + 1], psR[q % 2][:, 0:TG],
                                           ALU.mult, ALU.mult).then_inc(z_t, 1)
            for t in range(9):
                rows = P if t < 8 else NS
                dve.wait_ge(z_turn, t + 1)
                if t >= 2:
                    dve.wait_ge(z_out[t % 2], 16 * (t // 2))
                v.tensor_copy(yt[0:rows, t % 2, 512:D], psT[1][0:rows, :]).then_inc(z_c[1], 1)

        @block.gpsimd
        def _(pool):
            g_ = nc.gpsimd
            st = Steps(pool, pool_s)
            pool.sem_inc(ff_l, 2)
            st.link(g_.memset(ident[:], 0.0))
            g_.affine_select(out=ident[:], in_=ident[:], compare_op=ALU.not_equal, fill=1.0, base=0, pattern=[[-1, P]],
                             channel_multiplier=1).then_inc(ident_s, 1)
            pool.wait_ge(gpre_in, 16)
            for t in range(9):
                src, rows = (xin[t], P) if t < 8 else (xins, NS)
                pool.wait_ge(x_sq, t + 1)
                g_.tensor_tensor(src[0:rows, :], src[0:rows, :], g_pre[0:rows, :], ALU.mult).then_inc(x_g, 1)
            pool.wait_ge(small_in, 96)
            for g in range(4):
                g_.affine_select(out=wsg[:, g, :], in_=wsg[:, g, :], compare_op=ALU.is_ge, fill=0.0, base=0,
                                 pattern=[[-1, P]], channel_multiplier=1).then_inc(tril_s, 1)

            def keep(t, base_, pattern, mult):
                return g_.affine_select(out=t, in_=t, compare_op=ALU.is_ge, fill=NEG, base=base_, pattern=pattern,
                                        channel_multiplier=mult)
            g_.iota(iot[:], pattern=[[-1, 256]], base=P, channel_multiplier=1).then_inc(iota_s, 1)
            st.link(g_.memset(ones[:], 1.0))
            st.link(g_.memset(m_main[:], 0.0))
            st.link(keep(m_main[:], 3, [[-1, 7], [-4, P]], 4))
            st.link(keep(m_main[:], 125, [[1, 7], [4, P]], -4))
            st.link(g_.memset(m_edge[:], 0.0))
            st.link(keep(m_edge[:], -3, [[4, 32], [1, 7]], -4))
            st.link(g_.memset(m_far[:, 0, :], 0.0))
            st.link(keep(m_far[:, 0, :], P, [[-1, 256]], 1))
            st.link(keep(m_far[:, 0, :], 0, [[1, 256]], -1))
            pool.wait_ge(far_s, 1)
            keep(m_far[:, 1, :], P, [[-1, 256]], 1).then_inc(masks_s, 1)

            def queries(pair):
                def tile(i, t):
                    T = 8 * pair + 4 * i + t
                    pool.wait_ge(at_s, 2 * T + 1)
                    for e in range(2):
                        hd = slice(HD * e, HD * e + HD)
                        g_.tensor_copy(qst[hd, t % 2, e], qk[hd, 0:3, bass.ds(256 * (2 * i + t // 2) + P * (t % 2), P)]
                                       ).then_inc(at_q, 1)
                with pool.Fori(0, 2) as i:
                    for t in range(4):
                        tile(i, t)

            for pair in range(2):
                for tg in range(3):
                    pool.wait_ge(free[tg], M0[f"qkv{pair}"] + 10)
                if pair == 0:
                    pool.wait_ge(ln_lo, 9)
                    for tg in range(3):
                        pool.wait_ge(full[tg], M0["gb0"])
                    st.link(g_.memset(qst[:], 0.0))
                queries(pair)
            pool.wait_ge(kv_d, 16 * 64)
            pool.wait_ge(at_pv, 33)
            st.link(g_.memset(smask[:], 0.0))
            st.link(g_.affine_select(out=smask[:], in_=smask[:], compare_op=ALU.is_ge, fill=NEG, base=0,
                                     pattern=[[0, 3], [-4, NS]], channel_multiplier=1))
            g_.affine_select(out=smask[:], in_=smask[:], compare_op=ALU.is_ge, fill=NEG, base=3,
                             pattern=[[0, 3], [4, NS]], channel_multiplier=-1).then_inc(masks_s, 1)
            for k in range(24):
                pool.wait_ge(m_h, k + 1)
                g_.tensor_tensor(m_lo[:, k // 3, tgc[k % 3]], pt[:, 2 * (k % 2) + 1, :],
                                 m_hi[:, k // 3, tgc[k % 3]].bitcast(F32), ALU.subtract).then_inc(m_l, 1)
            for k in range(24):
                m, tg = k // 3, k % 3
                pool.wait_ge(free[tg], M0["wo"] + m + 2)
                y = y1[:, m, tgc[tg]]
                if m == 0:
                    g_.tensor_tensor(acc[:, tg, :], y, y, ALU.mult).then_inc(y1_a, 1)
                else:
                    pool.wait_ge(y1_a, k)
                    st.link(g_.tensor_tensor(sq[:, 0, :], y, y, ALU.mult))
                    g_.tensor_tensor(acc[:, tg, :], acc[:, tg, :], sq[:, 0, :], ALU.add).then_inc(y1_a, 1)
            for t in range(2):
                pool.wait_ge(xr_c[t], 9)
            for what, phase, tg in NORMS:
                if what == "chain":
                    continue
                for m in range(KD):
                    k = 8 * tg + m
                    if phase == 0:
                        pool.wait_ge(x1_t, k + 1)
                        part = xT[:, m, tgc[tg]]
                        g_.tensor_tensor(part, part, nt_[:, k % 3, :], ALU.add).then_inc(x1_s, 1)
                    else:
                        pool.wait_ge(f_h, k + 1)
                        g_.tensor_tensor(f_lo[:, m, tgc[tg]], nt_[:, (24 + k) % 3, :], f_hi[:, m, tgc[tg]].bitcast(F32),
                                         ALU.subtract).then_inc(f_l, 1)
            pool.wait_ge(full[2], M0["ffn"])
            g_.memset(y2[:], 0.0).then_inc(y2_z, 1)

            def a_low(j, tg, g3):
                pool.wait_ge(ff_h, g3 + 1)
                g_.tensor_tensor(a_lo[:, j, tgc[tg]], sq[:, (3 * j + tg) % 2, :], a_hi[:, j, tgc[tg]].bitcast(F32),
                                 ALU.subtract).then_inc(ff_l, 1)

            with pool.Fori(0, ROUNDS) as i:
                for j in range(FG):
                    for tg in range(3):
                        a_low(j, tg, 12 * i + 3 * j + tg)
            for j in range(2):
                for tg in range(3):
                    a_low(j, tg, 12 * ROUNDS + 3 * j + tg)
            for k in range(24):
                pool.wait_ge(y2_q, k + 1)
                if k < 3:
                    g_.tensor_scalar(acc[:, k, :], sq[:, k % 2, :], 1.0, 1.0, ALU.mult, ALU.mult).then_inc(y2_a, 1)
                else:
                    pool.wait_ge(y2_a, k)
                    g_.tensor_tensor(acc[:, k % 3, :], acc[:, k % 3, :], sq[:, k % 2, :], ALU.add).then_inc(y2_a, 1)
            for k in range(24):
                pool.wait_ge(z_t, k + 1)
                part = xT[:, k % 8, tgc[k // 8]]
                g_.tensor_tensor(part, part, nt_[:, k % 3, :], ALU.add).then_inc(z_s, 1)


_INS = ["x_prompt", "x_sample", "cache_win0", "cache_win1", "cache_win2", "g_mix_pre", "g_mix_post", "g_ffn_pre",
        "g_ffn_post", "w_in", "ln_v_g", "ln_v_b", "w_sg", "b_sg", "w_proj_attn", "w_proj_sg", "w_out", "w_gate",
        "w_up", "w_down"]
_OUTS = [("y_prompt", (1, SEQ, D)), ("y_sample", (NS, 1, D)),
         ("kv_prompt_g0", (1, 1, 128, 2, 4, HD)), ("kv_prompt_g1", (1, 1, 512, 2, 4, HD)),
         ("kv_prompt_g2", (1, 1, 1024, 2, 4, HD)), ("kv_sample_g0", (1, NS, 1, 2, 4, HD)),
         ("kv_sample_g1", (1, NS, 1, 2, 4, HD)), ("kv_sample_g2", (1, NS, 1, 2, 4, HD)),
         ("sg_v_sample", (1, NS, 1, SGW))]


def kernel(**inputs):
    import numpy as _np
    import concourse.bacc as _bacc
    from concourse.bass_utils import run_bass_kernel_spmd as _run

    nc = _bacc.Bacc("TRN2", target_bir_lowering=False, num_devices=1)
    arrays, A, O = {}, {}, {}
    for name in _INS:
        a = _np.ascontiguousarray(inputs[name])
        arrays[f"in_{name}"] = a
        A[name] = nc.dram_tensor(f"in_{name}", a.shape, mybir.dt.from_np(a.dtype), kind="ExternalInput").ap()
    for name, shape in _OUTS:
        O[name] = nc.dram_tensor(f"out_{name}", shape, F32, kind="ExternalOutput").ap()
    build(nc, A, O)
    r = _run(nc, [arrays], core_ids=[0])
    return tuple(r.results[0][f"out_{name}"] for name, _ in _OUTS)
```

```python
from contextlib import ExitStack

import concourse.bass as bass
from concourse import mybir

ALU = mybir.AluOpType
ACT = mybir.ActivationFunctionType
F32 = mybir.dt.float32
F32R = mybir.dt.float32r
BF16 = mybir.dt.bfloat16
I32 = mybir.dt.int32

P = 128
D = 1024
KD = D // P
SEQ = 1024
NS = 8
NT = SEQ + NS
TG = NT // 3
HD = 64
GROUPS = 3
AW = 768
SGW = 512
FF = 2816
KF = FF // P
U_COL = 3 * AW
GA_COL = 3 * AW + 2 * SGW
GB_COL = GA_COL + D
DIL = (1, 4, 16)
CKEYS = (128, 128, 32)
EPS = 1e-6
SCALE = HD ** -0.5
NEG = -1e30

STAGES = [("uv", 8, 8), ("qkv0", 9, 9), ("pb", 4, 8), ("gb0", 4, 4), ("qkv1", 9, 9), ("gb1", 4, 4),
          ("ga", 8, 8), ("pa", 2, 8), ("wo", 8, 8), ("ffn", 60, 80), ("tail", 6, 12)]
U0, M0 = {}, {}
_u = _m = 0
for _name, _nu, _nm in STAGES:
    U0[_name], M0[_name] = _u, _m
    _u += _nu
    _m += _nm
UNITS = _u
FG = 4
ROUNDS = KF // FG
WT = 6
X_TURNS = [(0, 2), (1, 0), (1, 2), (2, 0), (2, 2), (3, 0), (3, 2), (4, 0), (4, 2)]


def gate_chunks(n):
    return range(0, KD) if n == 0 else range(5 * n + 3, 5 * n + 8)


def gates_done(n):
    return [c // KD for c in gate_chunks(n) if c % KD == KD - 1]


class Steps:

    def __init__(self, eng, sem):
        self.eng, self.sem, self.n, self.term = eng, sem, 0, 0

    def mark(self, ins):
        ins.then_inc(self.sem, 1)
        self.n += 1

    def link(self, ins):
        ins.then_inc(self.sem, 1)
        self.n += 1
        self.eng.wait_ge(self.sem, self.term + self.n)

    def enter(self, i, per):
        self.start, self.per, self.term = self.n, per, i * per

    def leave(self, rounds):
        assert self.n - self.start == self.per, (self.n - self.start, self.per)
        self.n, self.term = self.start + self.per * rounds, 0


def build(nc, A, O):
    ctx = ExitStack()
    sem = lambda name: ctx.enter_context(nc.semaphore(name))
    base = (nc.sbuf_base + 31) // 32 * 32
    RB = KD * NT * 4
    R = [base + RB * i for i in range(5)]
    R4 = base + 4 * RB
    X = R4 + RB
    W = nc.sbuf_usable_end // 32 * 32 - 6 * 4096

    def at(name, shape, dt, off):
        n = 4 if dt in (F32, F32R, I32) else 2
        for s in shape[1:]:
            n *= s
        assert off + n <= nc.sbuf_usable_end, (name, off, n)
        return nc.alloc_sbuf_tensor_at(name, shape, dt, offset=off), off + (n + 31) // 32 * 32

    with ctx:
        w_raw = [at(f"w_raw{i}", [P, 8 * P], F32, W + 4096 * i)[0] for i in range(2)]
        w_hi = [at(f"w_hi{i}", [P, 8 * P], F32R, W + 4096 * (2 + i))[0] for i in range(2)]
        w_lo = [at(f"w_lo{i}", [P, 8 * P], F32R, W + 4096 * (4 + i))[0] for i in range(2)]
        h_hi, _ = at("h_hi", [P, KD, NT], F32R, R[0])
        h_lo, _ = at("h_lo", [P, KD, NT], F32R, R[1])
        xT, _ = at("xT", [P, KD, NT], F32, R[0])
        oa_hi, _o = at("oa_hi", [P, 2, NT], F32R, R[1])
        oa_lo, _o = at("oa_lo", [P, 2, NT], F32R, _o)
        pt, _o = at("pt", [P, 4, TG], F32, _o)
        f_hi, _ = at("f_hi", [P, KD, NT], F32R, R[1])
        mb, _ = at("mb", [P, KD, NT], F32, R[2])
        m_hi, _ = at("m_hi", [P, KD, NT], F32R, R[2])
        f_lo, _ = at("f_lo", [P, KD, NT], F32R, R[2])
        uv, _ = at("uv", [P, 8, NT], F32, R[3])
        ob_hi, _o = at("ob_hi", [P, 4, NT], F32R, R[3])
        ob_lo, _ = at("ob_lo", [P, 4, NT], F32R, _o)
        m_lo, _ = at("m_lo", [P, KD, NT], F32R, R[3])
        y2, _ = at("y2", [P, KD, NT], F32, R[3])
        g_pre, _o = at("g_pre", [P, D], F32, R[2])
        lnvg, _o = at("lnvg", [P, SGW], F32, _o)
        lnvb, _o = at("lnvb", [P, SGW], F32, _o)
        bsg, _o = at("bsg", [P, 4, P], F32, _o)
        wsg, _o = at("wsg", [P, 4, P], F32, _o)
        wsT, _o = at("wsT", [P, 4, P], F32, _o)
        vc, _o = at("vc", [P, 4, P], F32, _o)
        vt, _o = at("vt", [P, SGW], F32, _o)
        mixt, _o = at("mixt", [P, 4, P], F32, _o)
        w00, _o = at("w00", [NS, 8], F32, _o)
        vw, _o = at("vw", [NS, SGW], F32, _o)
        iot, _o = at("iot", [P, 256], I32, _o)
        iom, _o = at("iom", [P, 256], I32, _o)
        gpack, _o = at("gpack", [24, P], F32, _o)
        assert _o <= R[3]
        oaT, _o = at("oaT", [P, 2, NT], F32, R[3])
        pr, _o = at("pr", [P, 2, 1152], F32, _o)
        prT, _o = at("prT", [P, 9, P], F32, _o)
        qst1, _o = at("qst1", [P, 2, 2, GROUPS, P], F32, _o)
        otok, _o = at("otok", [P, 2, P], F32, _o)
        gt, _o = at("gt", [P, 2, TG], F32, _o)
        m_now, _o = at("m_now", [P, 4, P], BF16, _o)
        assert _o <= R[4]
        cv, _o = at("cv", [P, 24, 256], F32, R[3] + 2 * NT * 4)
        assert _o <= R[4]
        qk, _o = at("qk", [P, 6, NT], F32, R4)
        vtok, _o = at("vtok", [P, 25, P], F32, _o)
        kst, _ = at("kst", [P, 16, P], F32, _o)
        qst0, _ = at("qst0", [P, 2, 2, GROUPS, P], F32, _o)
        vT, VTO = at("vT", [P, GROUPS, NT], F32, _o)
        ga, _ = at("ga", [P, KD, NT], F32, R4)
        y1, _ = at("y1", [P, KD, NT], F32, R4)
        a_hi, _o = at("a_hi", [P, FG, NT], F32R, R4)
        a_lo, _ = at("a_lo", [P, FG, NT], F32R, _o)
        xin = [at(f"xin{i}", [P, D], F32, R4 + 4096 * i)[0] for i in range(8)]
        xins, _ = at("xins", [P, D], F32, X)
        m_main, _o = at("m_main", [P, 7, P], BF16, VTO)
        m_edge, _o = at("m_edge", [P, 32, 7], BF16, _o)
        m_far, _o = at("m_far", [P, 2, 256], BF16, _o)
        e_now, _o = at("e_now", [P, 32, 4], BF16, _o)
        ident, _o = at("ident", [P, P], F32, _o)
        ones, _o = at("ones", [P, P], F32, _o)
        gains, _o = at("gains", [P, 3, KD], F32, _o)
        sqkv, _o = at("sqkv", [P, 2, 9, NS], F32, _o)
        stat, _o = at("stat", [P, 64], F32, _o)
        assert _o <= W, (_o, W)
        kraw, _o = at("kraw", [P, 2, 256], F32, X)
        qb, _o = at("qb", [P, 2, 256], F32, _o)
        kq, _o = at("kq", [P, 2, 256], F32, _o)
        qz, _o = at("qz", [P, 2, 3, NS, 2], F32, _o)
        sst, _o = at("sst", [P, 2, 96], F32, _o)
        ssr, _o = at("ssr", [32, 320], F32, _o)
        spT, _o = at("spT", [P, 6, 32], F32, _o)
        smask, _o = at("smask", [32, 3, NS], F32, _o)
        svt, _o = at("svt", [NS, 3, 2, 256], F32, _o)
        assert _o <= VTO, (_o, VTO)
        qtok, _ = at("qtok", [NS, GROUPS, 256], F32, VTO)
        nt_, _o = at("nt_", [P, 3, TG], F32, X)
        sg, _ = at("sg", [P, NT], F32, _o)
        xre = [at(f"xre{i}", [P, D], F32, R[1] + 4096 * i)[0] for i in range(8)]
        xres, _ = at("xres", [P, D], F32, X)
        acc, _o = at("acc", [P, 3, TG], F32, X + 6 * TG * 4)
        diag, _o = at("diag", [P, 3, P], F32, _o)
        sq, _o = at("sq", [P, 2, TG], F32, _o)
        assert _o <= VTO, (_o, VTO)
        diag2, _ = at("diag2", [P, 3, P], F32, VTO)
        r2, _ = at("r2", [P, 3, TG], F32, X + 6 * TG * 4)
        yt, _ = at("yt", [P, 8, D], F32, R4)
        yts, _ = at("yts", [NS, D], F32, X)

        bank = [nc.alloc_psum_tensor(f"bank{i}", [P, 512], F32) for i in range(3)]
        psA = nc.alloc_psum_tensor("psA", [P, 512], F32)
        psB = nc.alloc_psum_tensor("psB", [P, 512], F32)
        psC = nc.alloc_psum_tensor("psC", [P, 512], F32)
        psT = [nc.alloc_psum_tensor(f"psT{i}", [P, 512], F32) for i in range(2)]
        psR = [psA, psB]
        Z_ORDER = (3, 4, 0, 1, 2, 5, 6, 7, 8)
        psZ = [psT, bank[0:2], psT, bank[0:2], psT, bank[0:2], [bank[2], psB], [psC, psT[0]], [psT[1], psA]]
        psK = psT + psR
        psX = [psT, psR]
        gbank, psO = bank[0:2], bank[2]

        q_rows = nc.dram_tensor("q_rows", (NS, AW), F32).ap()

        w_in_s = [sem(f"w_landed{i}") for i in range(2)]
        w_hi_s, w_lo_s = sem("w_hi_done"), sem("w_lo_done")
        full = [sem(f"bank_full{i}") for i in range(3)]
        free = [sem(f"bank_free{i}") for i in range(3)]
        dve_s, act_s, pool_s = sem("dve_step"), sem("act_step"), sem("pool_step")
        x_in = [sem(f"x_landed{i}") for i in range(9)]
        gpre_in, small_in, gains_in = sem("g_pre_landed"), sem("small_landed"), sem("gains_landed")
        ident_s, masks_s, gains_t, gains_s = sem("ident_done"), sem("masks_done"), sem("gains_turned"), sem("gains_done")
        x_sq, x_v, x_sd, x_g, x_h, x_t, x_hi, x_lo = [sem("x_" + s) for s in (
            "squared", "var", "sd", "gained", "scaled", "turned", "hi", "lo")]
        tril_s, ws_t, ws_c = sem("w_sg_masked"), sem("w_sg_turned"), sem("w_sg_copied")
        ln_u, ln_v, ln_t, ln_var, ln_sd, ln_n, ln_mix, ln_o, ln_hi, ln_lo, ln_w = [sem("ln_" + s) for s in (
            "gelu_u", "gelu_v", "turned", "var", "sd", "normalised", "mixed", "gated", "hi", "lo", "weighted")]
        sgv_out = sem("sg_v_stored")
        kv_t, kv_d = sem("kv_turned"), sem("kv_stored")
        kv_c = [sem("kv_copied_act"), sem("kv_copied_dve")]
        at_q, at_s, at_m, at_p, at_t0, at_t1, at_c0, at_c1, at_pv, at_o, at_ot, at_oc, at_gu = [sem("at_" + s) for s in (
            "query", "scores", "max", "probs", "turned0", "turned1", "copied0", "copied1", "pv", "otok", "oturned",
            "ocopied", "gated")]
        q_out = sem("s_query_stored")
        sk_in, sq_in = [[sem(f"{name}{i}") for i in range(2)] for name in ("k_cache_landed", "s_query_landed")]
        sv_in = sem("v_cache_landed")
        s_qz, s_kq, s_sc, s_self, s_sst, s_rows, s_ssr, s_exp, s_pn, s_pt, s_ptc, s_pv, s_oa, s_nt, s_nc, s_out = [
            sem("s_" + s) for s in ("queries", "k_times_q", "scores", "self", "scores_out", "rows", "rows_out",
                                    "exp", "probs", "probs_turned", "probs_out", "pv", "o_out", "new_turned", "new_out",
                                    "new_stored")]
        oa_h, oa_s, m_t, m_h, m_l = sem("oa_hi"), sem("oa_lo"), sem("m_sum"), sem("m_hi"), sem("m_lo")
        xr_in = [sem(f"x_again{i}") for i in range(9)]
        xr_t = sem("x_again_turned")
        xr_c = [sem("x_again_copied_act"), sem("x_again_copied_dve")]
        y1_q, y1_a = sem("y1_squared"), sem("y1_summed")
        n_s, n_v, n_sd, n_d, n_b = [[sem(f"norm{i}_{name}") for i in range(3)] for name in ("sum", "var", "sd", "diag", "spread")]
        r2_s = sem("norm1_copied")
        iota_s, far_s = sem("iota_done"), sem("m_far_started")
        x1_t, x1_s, x1_q, x1_a = sem("x1_term"), sem("x1_done"), sem("x1_squared"), sem("x1_summed")
        f_h, f_l = sem("f_hi"), sem("f_lo")
        ff_sg, ff_h, ff_l = sem("ff_silu"), sem("ff_hi"), sem("ff_lo")
        y2_q, y2_a = sem("y2_squared"), sem("y2_sq_summed")
        z_t, z_turn, z_out = sem("z_term"), sem("z_turned"), sem("z_stored")
        z_s = [sem("z_done_dve"), sem("z_done_pool")]
        z_c = [sem("z_copied_act"), sem("z_copied_dve")]

        block = ctx.enter_context(nc.Block())
        tgc = [slice(TG * t, TG * t + TG) for t in range(3)]
        NOFF = (0, P, TG - P)
        TILES_OF = (3, 6, 9)

        def chunks(w, r0, kc, c0, width):
            return w[r0:r0 + kc * P, bass.ds(c0, width)].rearrange("(k p) c -> p k c", p=P)

        @block.sync
        def _(sp):
            w_in = A["w_in"][0]

            def load_w(u, par, src, kc):
                if not isinstance(u, int) or u >= 2:
                    sp.wait_ge(w_lo_s, u - 1)
                sp.dma_start(w_raw[par][:].rearrange("p (k c) -> p k c", k=kc), src).then_inc(w_in_s[par], 16)

            xp = A["x_prompt"][0].rearrange("(t p) d -> t p d", p=P)
            xs = A["x_sample"].rearrange("b s d -> (b s) d")
            for t in range(8):
                sp.dma_start(xin[t][:], xp[t]).then_inc(x_in[t], 16)
                if t in (2, 3):
                    load_w(t - 2, t - 2, chunks(w_in, 0, 8, U_COL + P * (t - 2), P), 8)
            sp.dma_start(xins[0:NS, :], xs).then_inc(x_in[8], 16)
            for j, n in enumerate(("g_mix_post", "g_ffn_pre", "g_ffn_post")):
                sp.dma_start(gpack[8 * j:8 * j + 8, :], A[n][0].rearrange("(k p) -> k p", p=P)).then_inc(gains_in, 16)
            sp.dma_start(lnvg[:], A["ln_v_g"][0:1, :].broadcast_to([P, SGW])).then_inc(small_in, 16)
            sp.dma_start(lnvb[:], A["ln_v_b"][0:1, :].broadcast_to([P, SGW])).then_inc(small_in, 16)
            sp.dma_start(bsg[:].rearrange("p g t -> p (g t)"),
                         A["b_sg"].rearrange("l g t -> l (g t)").broadcast_to([P, SGW])).then_inc(small_in, 16)
            sp.dma_start(wsg[:], A["w_sg"][0].rearrange("g t s -> t g s")).then_inc(small_in, 16)
            with nc.allow_non_contiguous_dma("8 x 8 numbers"):
                sp.dma_start(w00[:, 0:4], A["w_sg"][0][:, 0, 0:1].rearrange("g o -> o g").broadcast_to([NS, 4])
                             ).then_inc(small_in, 16)
                sp.dma_start(w00[:, 4:8], A["b_sg"][0][:, 0:1].rearrange("g o -> o g").broadcast_to([NS, 4])
                             ).then_inc(small_in, 16)
            with sp.Fori(1, 4) as i:
                for j in range(2):
                    load_w(2 * i + j, j, chunks(w_in, 0, 8, U_COL + P * (2 * i + j), P), 8)

            def load_qkv(pair):
                for j in range(9):
                    u = U0[f"qkv{pair}"] + j
                    load_w(u, u % 2, chunks(w_in, 0, 8, AW * (j // 3) + 256 * (j % 3) + P * pair, P), 8)

            def store_kv(pair):
                sp.wait_ge(kv_c[0], 6 * (pair + 1))
                sp.wait_ge(kv_c[1], 5 * (pair + 1))
                for g, name in enumerate(("kv_prompt_g0", "kv_prompt_g1", "kv_prompt_g2")):
                    for kv in range(2):
                        dst = O[name][0, 0, :, kv, 2 * pair:2 * pair + 2, :].rearrange("s h d -> s (h d)")
                        src = vtok if kv else kst
                        for half in ((0, 1) if g == 2 else (1,)):
                            for r in range(4):
                                if kv:
                                    tile = 4 + r if g == 0 else 9 + 8 * (g - 1) + 4 * half + r
                                else:
                                    tile = 4 * g + r if g < 2 else 8 + 4 * half + r
                                if g == 0:
                                    sp.dma_start(dst[r:P:4, :], src[96:128, tile, :]).then_inc(kv_d, 16)
                                else:
                                    first = 512 * half if g == 2 else 0
                                    sp.dma_start(dst[first + r:first + 512:4, :], src[:, tile, :]).then_inc(kv_d, 16)

            load_qkv(0)
            for i in range(4):
                u = U0["pb"] + i
                load_w(u, u % 2, chunks(A["w_proj_sg"][0], 0, 4, 256 * i, 256), 4)
                if i == 1:
                    sp.wait_ge(ln_n, 9)
                    sp.dma_start(O["sg_v_sample"][0, :, 0, :], vt[0:NS, :]).then_inc(sgv_out, 16)
            store_kv(0)
            for i in range(4):
                u = U0["gb0"] + i
                load_w(u, u % 2, chunks(w_in, 0, 8, GB_COL + P * i, P), 8)
            load_qkv(1)
            for i in range(4):
                u = U0["gb1"] + i
                load_w(u, u % 2, chunks(w_in, 0, 8, GB_COL + P * (4 + i), P), 8)
                if i == 1:
                    store_kv(1)

            def load_k(kk):
                n, g = kk // 3, kk % 3
                ck = CKEYS[g]
                rows = A[f"cache_win{g}"][0, n].rearrange("(s r) k h d -> s r k (h d)", r=DIL[g])[:, 0]
                if kk >= 2:
                    sp.wait_ge(s_kq, kk - 1)
                sp.dma_start(kraw[0:ck, kk % 2, :], rows[:, 0, :]).then_inc(sk_in[kk % 2], 16)
                sp.dma_start(qb[0:ck, kk % 2, :], q_rows[n:n + 1, 256 * g:256 * g + 256].broadcast_to([ck, 256])).then_inc(sq_in[kk % 2], 16)
                sp.dma_start(cv[0:ck, kk, :], rows[:, 1, :]).then_inc(sv_in, 16)

            for i in range(8):
                u = U0["ga"] + i
                load_w(u, u % 2, chunks(w_in, 0, 8, GA_COL + P * i, P), 8)
                if i == 1:
                    sp.wait_ge(at_oc, 17)
                    sp.wait_ge(at_gu, 26)
                    sp.wait_ge(kv_d, 16 * 64)
                    sp.wait_ge(s_nc, 5)
                    sp.dma_start(q_rows, qtok[:].rearrange("b g c -> b (g c)")).then_inc(q_out, 16)
                    sp.wait_ge(q_out, 16)
                if 1 <= i < 6:
                    for kk in range(5 * i - 5, min(5 * i, 24)):
                        load_k(kk)
            for g in range(GROUPS):
                sp.dma_start(O[f"kv_sample_g{g}"][0, :, 0].rearrange("b k h d -> b (k h d)"),
                             svt[:, g].rearrange("b k c -> b (k c)")).then_inc(s_out, 16)
            for i in range(2):
                u = U0["pa"] + i
                load_w(u, u % 2, chunks(A["w_proj_attn"][0], 0, 2, 512 * i, 512), 2)

            def x_again(t):
                rows, dst = (P, xre[t]) if t < 8 else (NS, xres)
                sp.dma_start(dst[0:rows, :], xp[t] if t < 8 else xs).then_inc(xr_in[t], 16)

            for i in range(8):
                u = U0["wo"] + i
                load_w(u, u % 2, chunks(A["w_out"][0], 0, 8, P * i, P), 8)
                if i == 1:
                    sp.wait_ge(m_l, 24)
                if 1 <= i < 4:
                    for t in range(3 * i - 3, 3 * i):
                        x_again(t)
            wg, wu, wd = A["w_gate"][0], A["w_up"][0], A["w_down"][0]
            with sp.Fori(0, ROUNDS) as i:
                for j in range(FG):
                    u = U0["ffn"] + 12 * i + 2 * j
                    load_w(u, 0, chunks(wg, 0, 8, 512 * i + P * j, P), 8)
                    load_w(u + 1, 1, chunks(wu, 0, 8, 512 * i + P * j, P), 8)
                for j in range(4):
                    u = U0["ffn"] + 12 * i + 8 + j
                    load_w(u, j % 2, wd[bass.ds(512 * i, 512), 256 * j:256 * j + 256].rearrange("(k p) c -> p k c", p=P), 4)
            u = U0["tail"]
            for j in range(2):
                load_w(u + 2 * j, 0, chunks(wg, 0, 8, 512 * ROUNDS + P * j, P), 8)
                load_w(u + 2 * j + 1, 1, chunks(wu, 0, 8, 512 * ROUNDS + P * j, P), 8)
            for j in range(2):
                load_w(u + 4 + j, j, chunks(wd, 512 * ROUNDS, 2, 512 * j, 512), 2)
            yp = O["y_prompt"][0].rearrange("(t p) d -> t p d", p=P)
            for q, t in enumerate(Z_ORDER):
                sp.wait_ge(z_c[0], min(2 * q + 2, q + 6))
                if q >= 5:
                    sp.wait_ge(z_c[1], q - 4)
                dst, src = (yp[t], yt[:, t, :]) if t < 8 else (O["y_sample"].rearrange("b s d -> (b s) d"), yts[:])
                sp.dma_start(dst, src).then_inc(z_out, 16)
            sp.wait_ge(z_out, 144)
            sp.wait_ge(kv_d, 16 * 64)
            sp.wait_ge(s_out, 48)
            sp.wait_ge(sgv_out, 16)

        @block.tensor
        def _(pe):
            mm = nc.tensor.matmul

            def turn(out, in_):
                k = in_.shape[0]
                return nc.tensor.transpose(out, in_, ident[0:k, 0:k])

            def product3(out, par, ws, hi, lo, k, tg, first, last):
                mm(out[:, 0:TG], w_hi[par][:, ws], hi[:, k, tgc[tg]], start=first, stop=False)
                mm(out[:, 0:TG], w_hi[par][:, ws], lo[:, k, tgc[tg]], start=False, stop=False)
                return mm(out[:, 0:TG], w_lo[par][:, ws], hi[:, k, tgc[tg]], start=False, stop=last)

            def job(m, par, b, tg, kc, width, hi, lo, out=None, wait=True, aside=None):
                if wait:
                    pe.wait_ge(free[tg], m + 1)
                for k in range(kc):
                    if aside and k in aside:
                        aside[k]()
                    ws = slice(width * k + P * b, width * k + P * b + P)
                    ins = product3(out or bank[tg], par, ws, hi, lo, k, tg, k == 0, k == kc - 1)
                return ins.then_inc(full[tg], 1)

            def unit(u, m, par, kc, hi, lo, before=None, after=None, aside=None):
                pe.wait_ge(w_lo_s, u + 1)
                mb_ = 8 // kc
                for b in range(mb_):
                    for tg in range(3):
                        if before and b == 0:
                            before(tg)
                        job(m + b, par, b, tg, kc, P * mb_, hi, lo, aside=aside(tg) if aside else None)
                        if after:
                            after(b, tg)

            def pair(U, M, hi, lo, after_pair, before=None, aside={}):
                for n in range(6):
                    tg, j = n // 2, n % 2
                    if tg == 0:
                        pe.wait_ge(w_lo_s, U + j + 1)
                    if before and j == 0:
                        before(tg)
                    if n >= 3:
                        pe.wait_ge(free[(n - 3) // 2], M + (n - 3) % 2 + 2)
                    elif after_pair:
                        pe.wait_ge(free[(n + 3) // 2], M - 2 + (n + 3) % 2 + 2)
                    else:
                        pe.wait_ge(free[n], M + 1)
                    job(M + j, (U + j) % 2, 0, tg, 8, P, hi, lo, bank[n % 3], wait=False, aside=aside.get(n))

            def after_pair(M):
                return lambda tg: pe.wait_ge(free[(3 + tg) // 2], M + (3 + tg) % 2 + 2)

            pe.sem_inc(at_s, 3)
            pe.sem_inc(at_t1, 2)
            pe.sem_inc(at_pv, 1)
            pe.sem_inc(at_ot, 2)
            pe.wait_ge(ident_s, 1)

            def first_job(n):
                tg, j = n // 2, n % 2
                pe.wait_ge(w_lo_s, j + 1)
                if j == 0:
                    pe.wait_ge(x_lo, TILES_OF[tg])
                if n >= 3:
                    pe.wait_ge(free[(n - 3) // 2], (n - 3) % 2 + 2)
                job(j, j, 0, tg, 8, P, h_hi, h_lo, bank[n % 3], wait=False)

            for step in (0, 1, 2, 3, "a", 4, "b", 5, 6, "c", 7, 8, "d", "e", "f"):
                if isinstance(step, str):
                    first_job("abcdef".index(step))
                    continue
                t = step
                src, rows = (xin[t], P) if t < 8 else (xins, NS)
                pe.wait_ge(x_h, t + 1)
                if t >= 2:
                    pe.wait_ge(x_lo, t - 1)
                for k in range(KD):
                    ins = turn(psX[t % 2][k // 4][:, P * (k % 4):P * (k % 4) + rows], src[0:rows, P * k:P * k + P])
                ins.then_inc(x_t, 1)
            pe.wait_ge(gains_in, 48)
            turn(psC[:, 0:24], gpack[:, :]).then_inc(gains_t, 1)
            pe.wait_ge(tril_s, 4)
            for g in range(4):
                ins = turn(psT[0][:, P * g:P * g + P], wsg[:, g, :])
            ins.then_inc(ws_t, 1)

            for tg in range(3):
                pe.wait_ge(free[tg], 3)
            with pe.Fori(1, 4) as i:
                for j in range(2):
                    unit(2 * i + j, 2 * i + j, j, 8, h_hi, h_lo)

            def kv_turns(pair):
                for tg in range(3):
                    pe.wait_ge(free[tg], M0[f"qkv{pair}"] + 10)
                n = 0
                tiles = []
                for g in range(GROUPS):
                    tiles += [vT[:, g, 512 * hh + r:512 * hh + 512:4] for hh in range(2) for r in range(4)]
                    if g == 0:
                        tiles.append(vT[:, 0, 384:512])
                lots = [tiles[4 * a:4 * a + 4] for a in range(7)]
                keys = [qk[:, 3 + g, 256 * r + 128:256 * r + 256] for g in range(2) for r in range(4)]
                keys += [qk[:, 5, 256 * r + 128 * hh:256 * r + 128 * hh + 128] for hh in range(2) for r in range(4)]
                lots += [keys[4 * a:4 * a + 4] for a in range(4)]
                for a, lot in enumerate(lots):
                    if a == 2 and pair == 0:
                        pe.wait_ge(ln_o, 9)
                    if a >= 4:
                        pe.wait_ge(kv_c[a % 2], (6 if a % 2 == 0 else 5) * pair + a // 2 - 1)
                    for b, src in enumerate(lot):
                        ins = turn(psK[a % 4][:, P * b:P * b + P], src)
                    ins.then_inc(kv_t, 1)

            def ln_turn(c):
                n = P if c < 8 else NS
                pe.wait_ge(ln_v, c + 1)
                if c == 0:
                    pe.wait_ge(ws_c, 1)
                for g in range(4):
                    ins = turn(psT[0][0:n, P * g:P * g + P], vc[:, g, 0:n])
                ins.then_inc(ln_t, 1)

            def ln_mixing(c):
                if c == 0:
                    pe.wait_ge(ws_c, 1)
                if c < 8:
                    pe.wait_ge(ln_n, c + 1)
                    if c:
                        pe.wait_ge(ln_o, c)
                    for g in range(4):
                        ins = mm(psA[:, P * g:P * g + P], vt[:, P * g:P * g + P], wsT[:, g, :], start=True, stop=True)
                else:
                    pe.wait_ge(ln_w, 1)
                    pe.wait_ge(ln_o, 8)
                    for g in range(4):
                        ins = turn(psA[:, P * g:P * g + NS], vw[:, P * g:P * g + P])
                ins.then_inc(ln_mix, 1)

            for j in range(9):
                u, m = U0["qkv0"] + j, M0["qkv0"] + j

                def after(b, tg, j=j):
                    if tg == 0:
                        ln_turn(j)
                    if tg == 2:
                        ln_mixing(j)
                unit(u, m, u % 2, 8, h_hi, h_lo, after=after)
            kv_turns(0)
            pe.wait_ge(ln_lo, 9)
            with pe.Fori(0, 2) as i:
                for j in range(2):
                    unit(U0["pb"] + 2 * i + j, M0["pb"] + 4 * i + 2 * j, (U0["pb"] + j) % 2, 4, ob_hi, ob_lo)

            def attention(pair, U, M):
                qst = (qst0, qst1)[pair]

                def scores(i, n):
                    r, hh, e = 2 * i + n // 4, n // 2 % 2, n % 2
                    N, T = 16 * pair + 8 * i + n, 8 * pair + 4 * i + n // 2
                    pe.wait_ge(at_q, 2 * T + 2)
                    pe.wait_ge(at_m, N + 1)
                    kr = qk[:, 3, 0:SEQ].rearrange("p (c i) -> p c i", c=4)
                    w = P * (hh + 1)
                    mm(psA[:, :].rearrange("p (c i) -> p c i", c=4), qst[:, hh, e, 0, :], kr[:, :, P * hh:P * hh + P],
                       start=True, stop=True)
                    if hh:
                        mm(psC[:, 0:P].rearrange("p (i c) -> p i c", c=4), qst[:, hh, e, 0, :],
                           kr.rearrange("p c i -> p i c")[:, 96:128, :], start=True, stop=True)
                    for g in (1, 2):
                        ins = mm(psB[:, w * (g - 1):w * g], qst[:, hh, e, g, :], qk[:, 3 + g, bass.ds(256 * r, w)],
                                 start=True, stop=True)
                    ins.then_inc(at_s, 1)

                def turns(i, n):
                    N, nb = 16 * pair + 8 * i + n, 9 if n // 2 % 2 else 6
                    pe.wait_ge(at_p, N + 1)
                    pe.wait_ge(at_c0, N + 1)
                    pe.wait_ge(at_c1, N + 1)
                    for b in range(nb):
                        if b == 8:
                            pe.wait_ge(at_o, N + 1)
                            pe.wait_ge(at_oc, 8 * pair + 4 * i + n // 2 + 1)
                        out = psO[:, 256:384] if b == 8 else psT[b // 4][:, P * (b % 4):P * (b % 4) + P]
                        ins = turn(out, pr[:, n % 2, P * b:P * b + P])
                        if b == 3:
                            ins.then_inc(at_t0, 1)
                    ins.then_inc(at_t1, 1)

                def pv(i, n):
                    r, hh, e = 2 * i + n // 4, n // 2 % 2, n % 2
                    N = 16 * pair + 8 * i + n
                    hd = slice(HD * e, HD * e + HD)
                    pe.wait_ge(at_c0, N + 2)
                    pe.wait_ge(at_c1, N + 2)
                    pe.wait_ge(at_o, N + 1)
                    pe.wait_ge(at_oc, 8 * pair + 4 * i + n // 2 + 1)
                    values = [vtok[:, 4 * hh + c, hd] for c in range(4)]
                    for g in (1, 2):
                        values += [vtok[:, 9 + 8 * (g - 1) + 4 * q + r, hd] for q in range(hh + 1)]
                    if hh:
                        values.append(vtok[:, 8, hd])
                    for b, v in enumerate(values):
                        ins = mm(psO[:, P:P + HD], prT[:, b, :], v, start=(b == 0), stop=(b == len(values) - 1))
                    ins.then_inc(at_pv, 1)

                def oturn(i, t):
                    T = 8 * pair + 4 * i + t
                    pe.wait_ge(at_o, 2 * T + 3)
                    pe.wait_ge(at_oc, T + 1)
                    turn(psO[:, 384:512], otok[:, t % 2, :]).then_inc(at_ot, 1)

                def gates(i, n):
                    for c in gate_chunks(n):
                        q, k = c // KD, c % KD
                        if k == 0:
                            if q % 3 == 0:
                                pe.wait_ge(w_lo_s, U + 2 * i + q // 3 + 1)
                            pe.wait_ge(free[q % 3], M + 2 * i + q // 3 + 1)
                            pe.wait_ge(free[(q - 2) % 3], M + 2 * i + (q - 2) // 3 + 2)
                        ins = product3(gbank[q % 2], (U + q // 3) % 2, slice(P * k, P * k + P), h_hi, h_lo, k, q % 3,
                                       k == 0, k == KD - 1)
                        if k == KD - 1:
                            ins.then_inc(full[q % 3], 1)

                pe.wait_ge(kv_c[0], 6 * (pair + 1))
                pe.wait_ge(kv_c[1], 5 * (pair + 1))
                pe.wait_ge(free[2], M + 1)
                with pe.Fori(0, 2) as i:
                    scores(i, 0)
                    gates(i, 0)
                    for n in range(1, 9):
                        if n < 8:
                            scores(i, n)
                        if n in (3, 5, 7):
                            oturn(i, (n - 3) // 2)
                        turns(i, n - 1)
                        gates(i, n)
                        pv(i, n - 1)
                    oturn(i, 3)
                pe.wait_ge(at_oc, 8 * pair + 9)
                for tg in range(3):
                    pe.wait_ge(free[tg], M + 5)

            attention(0, U0["gb0"], M0["gb0"])
            for j in range(9):
                u = U0["qkv1"] + j
                unit(u, M0["qkv1"] + j, u % 2, 8, h_hi, h_lo)
            kv_turns(1)
            attention(1, U0["gb1"], M0["gb1"])

            def sample_step(j, tg):
                if j == 0 and tg == 0:
                    for g in range(GROUPS):
                        for p in range(2):
                            for kv in range(2):
                                c = 256 * kv + P * p
                                turn([psA, psB, psC][g][0:NS, c:c + P], sqkv[:, p, 3 + 3 * kv + g, :])
                            c = 256 * (g % 2) + P * p
                            ins = turn(psT[g // 2][0:NS, c:c + P], sqkv[:, p, g, :])
                    ins.then_inc(s_nt, 1)
                elif j == 5 and tg == 0:
                    pe.wait_ge(s_nc, 5)
                    pe.wait_ge(s_qz, 1)
                    for g in range(GROUPS):
                        for p in range(2):
                            out = psB[0:NS, 32 * g:32 * g + 32].rearrange("k (n s) -> k n s", s=4)[:, :, 2 * p:2 * p + 2]
                            ins = mm(out, sqkv[:, p, 3 + g, :], qz[:, p, g], start=True, stop=True)
                    ins.then_inc(s_self, 1)
                elif j == 5 and tg == 1:
                    pe.wait_ge(s_sst, 1)
                    pe.wait_ge(s_sc, 24)
                    turn(psC[0:32, 0:128], sst[:, 0, 0:32])
                    turn(psC[0:32, 128:256], sst[:, 0, 32:64])
                    turn(psC[0:32, 256:288], sst[0:32, 0, 64:96])
                    for g in range(GROUPS):
                        ins = turn(psC[0:32, 288 + 8 * g:296 + 8 * g], sst[0:NS, 1, 32 * g:32 * g + 32])
                    ins.then_inc(s_rows, 1)
                elif j == 6 and tg == 0:
                    pe.wait_ge(s_pn, 1)
                    turn(psA[:, 0:32], ssr[:, 0:128])
                    turn(psA[:, 32:64], ssr[:, 128:256])
                    turn(psA[0:32, 64:96], ssr[:, 256:288])
                    for g in range(GROUPS):
                        ins = turn(psA[0:NS, 96 + 32 * g:128 + 32 * g], ssr[:, 288 + 8 * g:296 + 8 * g])
                    ins.then_inc(s_pt, 1)

            def sample_pv(c):
                if c == 0:
                    pe.wait_ge(s_ptc, 3)
                for p in range(2):
                    if c < GROUPS:
                        out = psB[:, 16 * p:16 * p + 16].rearrange("k (n e) -> k n e", e=2)
                        w = spT[0:NS, 3 + c, :].rearrange("k (n s) -> k n s", s=4)[:, :, 2 * p:2 * p + 2]
                        mm(out, svt[:, c, 1, P * p:P * p + P], w, start=(c + p == 0), stop=False, skip_group_check=True)
                        continue
                    if c == GROUPS and p == 0:
                        pe.wait_ge(sv_in, 16 * 24)
                    kk = c - GROUPS
                    n, g = kk // 3, kk % 3
                    ck = CKEYS[g]
                    ins = mm(psB[:, 16 * p + 2 * n:16 * p + 2 * n + 2], cv[0:ck, kk, P * p:P * p + P],
                             spT[0:ck, g, 4 * n + 2 * p:4 * n + 2 * p + 2], start=False,
                             stop=(kk == 23 and p == 1), skip_group_check=True)
                    if kk == 23 and p == 1:
                        ins.then_inc(s_pv, 1)

            def pv_aside(j, tg):
                first = 24 * (j - 6) + 8 * tg - 12
                return {k: (lambda c=first + k: sample_pv(c)) for k in range(8) if 0 <= first + k < 27} if j >= 6 else None

            for j in range(8):
                u = U0["ga"] + j
                unit(u, M0["ga"] + j, u % 2, 8, h_hi, h_lo, after=lambda b, tg, j=j: sample_step(j, tg),
                     aside=lambda tg, j=j: pv_aside(j, tg))
            for j in range(2):
                u = U0["pa"] + j
                unit(u, M0["pa"] + 4 * j, u % 2, 2, oa_hi, oa_lo, before=lambda tg: pe.wait_ge(oa_s, tg + 1))

            def x_turn(t):
                src, rows = (xre[t], P) if t < 8 else (xres, NS)
                pe.wait_ge(xr_in[t], 16)
                if t:
                    pe.wait_ge(xr_c[0], t)
                    pe.wait_ge(xr_c[1], t)
                for k in range(KD):
                    ins = turn(psT[k // 4][:, P * (k % 4):P * (k % 4) + rows], src[0:rows, P * k:P * k + P])
                ins.then_inc(xr_t, 1)

            for j in range(WT):
                u = U0["wo"] + j

                def after(b, tg, j=j):
                    if (j, tg) in X_TURNS:
                        x_turn(X_TURNS.index((j, tg)))
                unit(u, M0["wo"] + j, u % 2, 8, m_hi, m_lo, after=after,
                     before=(lambda tg: pe.wait_ge(m_l, 21 + tg + 1)) if j == 0 else None)

            sums = [psT[0], psC, psC]

            def norm_sum(phase, tg):
                s, done = ((y1_a, 3 * WT + 2 * tg + 2), (x1_a, 8 * (tg + 1)), (y2_a, 8 * (tg + 1)))[phase]
                pe.wait_ge(s, done)
                if tg:
                    pe.wait_ge(n_v[phase], tg)
                elif phase == 0:
                    pe.wait_ge(xr_c[0], 9)
                    pe.wait_ge(xr_c[1], 9)
                for j in range(3):
                    ins = mm(sums[phase][:, j:j + 1], acc[:, tg, NOFF[j]:NOFF[j] + P], ones[:, 0:1], start=True, stop=True)
                ins.then_inc(n_s[phase], 1)

            def norm_spread(phase, tg):
                pe.wait_ge(n_d[phase], tg + 1)
                if phase == 1 and tg:
                    pe.wait_ge(r2_s, tg)
                if phase != 1 and tg == 2:
                    pe.wait_ge(z_t if phase else x1_t, 8)
                for j in range(3):
                    ins = mm((psT[1] if phase == 1 else psR[tg % 2])[:, NOFF[j]:NOFF[j] + P], ones[:, :],
                             (diag2 if phase == 1 else diag)[:, j, :], start=True, stop=True)
                ins.then_inc(n_b[phase], 1)

            pair(U0["wo"] + WT, M0["wo"] + WT, m_hi, m_lo, False, aside={
                2: {6: lambda: norm_sum(0, 0)},
                3: {3: lambda: norm_spread(0, 0)},
                5: {4: lambda: norm_sum(0, 1)}})

            def f_ready(tg):
                norm_sum(1, tg)
                if tg < 2:
                    norm_spread(0, tg + 1)
                pe.wait_ge(f_l, 8 * (tg + 1))

            def ffn_round(i):
                first = isinstance(i, int)
                if first:
                    pair(U0["ffn"], M0["ffn"], f_hi, f_lo, True, f_ready, {
                        0: {1: lambda: norm_spread(1, 0)}, 1: {4: lambda: norm_sum(0, 2)},
                        2: {1: lambda: norm_spread(1, 1)}, 4: {1: lambda: norm_spread(1, 2)}})
                for j in range(2 if first else 0, 2 * FG):
                    unit(U0["ffn"] + 12 * i + j, M0["ffn"] + 16 * i + j, j % 2, 8, f_hi, f_lo,
                         before=after_pair(M0["ffn"]) if first and j == 2 else None)
                for j in range(4):
                    unit(U0["ffn"] + 12 * i + 8 + j, M0["ffn"] + 16 * i + 8 + 2 * j, j % 2, 4, a_hi, a_lo,
                         before=(lambda tg: pe.wait_ge(ff_l, 12 * i + 9 + tg + 3)) if j == 0 else None)
            ffn_round(0)
            with pe.Fori(1, ROUNDS) as i:
                ffn_round(i)
            for j in range(4):
                unit(U0["tail"] + j, M0["tail"] + j, j % 2, 8, f_hi, f_lo)
            M = M0["tail"] + 4
            for n in range(24):
                tg, b = n // 8, n % 8
                if n in (0, 4):
                    pe.wait_ge(w_lo_s, U0["tail"] + 5 + n // 4)
                if b == 0:
                    pe.wait_ge(ff_l, 12 * ROUNDS + 3 + tg + 3)
                if n >= 3:
                    pe.wait_ge(free[(n - 3) // 8], M + (n - 3) % 8 + 2)
                else:
                    pe.wait_ge(free[n], M + 1)
                if n in (12, 20):
                    norm_sum(2, n // 12 - 1 if n == 12 else 1)
                if n == 16:
                    norm_spread(2, 0)
                job(M + b, b // 4, b % 4, tg, 2, 4 * P, a_hi, a_lo, bank[n % 3], wait=False)
            norm_spread(2, 1)
            norm_sum(2, 2)
            norm_spread(2, 2)
            def z_turn_tile(q, ks=range(KD)):
                t = Z_ORDER[q]
                rows = P if t < 8 else NS
                for k in ks:
                    ins = turn(psZ[q][k // 4][0:rows, P * (k % 4):P * (k % 4) + P], xT[:, k, P * t:P * t + rows])
                return ins

            for q in range(5):
                pe.wait_ge(z_s[0], 8)
                if q >= 2:
                    pe.wait_ge(z_s[1], 8)
                    pe.wait_ge(z_c[0], 2 * q - 2)
                z_turn_tile(q).then_inc(z_turn, 1)
            pe.wait_ge(z_c[0], 10)
            for k in range(KD):
                pe.wait_ge(z_s[0], 9 + k if k < 6 else 14)
                if k >= 6:
                    pe.wait_ge(z_s[1], 3 + k)
                for q in range(5, 8):
                    ins = z_turn_tile(q, [k])
                    if k == KD - 1:
                        ins.then_inc(z_turn, 1)
            z_turn_tile(8).then_inc(z_turn, 1)

        def by4(ps, n=P):
            return ps[:, :].rearrange("p (k n) -> p k n", k=4)[:, :, 0:n]

        @block.scalar
        def _(act):
            fn = nc.scalar.activation
            act.dma_start(g_pre[:], A["g_mix_pre"][0:1, :].broadcast_to([P, D])).then_inc(gpre_in, 16)
            act.sem_inc(at_c0, 1)
            act.sem_inc(at_oc, 1)

            def split(u, par, m_used):
                act.wait_ge(w_in_s[par], 16 * (u // 2 + 1) if isinstance(u, int) else u)
                if m_used is not None:
                    act.wait_ge(full[2], m_used)
                fn(w_hi[par][:], w_raw[par][:], ACT.Copy).then_inc(w_hi_s, 1)

            def split_in(u0, per, i, j, m_used):
                u = u0 + j + 2
                par = u % 2
                if isinstance(i, int):
                    u += per * i
                    if u < UNITS:
                        split(u, par, m_used)
                    return
                act.wait_ge(w_in_s[par], 16 * (u // 2 + 1) + 8 * per * i)
                act.wait_ge(full[2], m_used)
                fn(w_hi[par][:], w_raw[par][:], ACT.Copy).then_inc(w_hi_s, 1)

            def square(t):
                src, rows = (xin[t], P) if t < 8 else (xins, NS)
                act.wait_ge(x_in[t], 16)
                if t >= 6:
                    act.wait_ge(x_sq, t - 5)
                fn(uv[0:rows, 2 + t % 6, 0:D], src[0:rows, :], ACT.Square, accum_out=stat[0:rows, t:t + 1]).then_inc(x_sq, 1)

            def x_high(t):
                n = P if t < 8 else NS
                act.wait_ge(x_t, t + 1)
                for a in range(2):
                    fn(h_hi[:, 4 * a:4 * a + 4, P * t:P * t + n], by4(psX[t % 2][a], n), ACT.Copy).then_inc(x_hi, 1)

            def first_copies(tg, js=(0, 1)):
                for j in js:
                    act.wait_ge(full[tg], j + 1)
                    fn(uv[:, j, tgc[tg]], bank[(2 * tg + j) % 3][:, 0:TG], ACT.Copy).then_inc(free[tg], 1)

            def rms(t):
                rows = P if t < 8 else NS
                act.wait_ge(x_v, t + 1)
                fn(stat[0:rows, 18 + t:19 + t], stat[0:rows, 9 + t:10 + t], ACT.Sqrt).then_inc(x_sd, 1)

            square(0)
            rms(0)
            square(1)
            for t in range(9):
                if t < 7:
                    square(t + 2)
                if t < 8:
                    rms(t + 1)
                if t:
                    x_high(t - 1)
                if t in (2, 3):
                    split(t - 2, t - 2, None)
                if t == 6:
                    first_copies(0)
            x_high(8)
            first_copies(1)
            first_copies(2, [0])
            split_in(0, 2, 0, 0, 1)
            first_copies(2, [1])
            split_in(0, 2, 0, 1, 2)
            act.wait_ge(gains_t, 1)
            fn(gains[:, :, :].rearrange("p a k -> p (a k)"), psC[:, 0:24], ACT.Copy).then_inc(gains_s, 1)
            act.wait_ge(ws_t, 1)
            fn(wsT[:, :, :].rearrange("p g t -> p (g t)"), psT[0][:, :], ACT.Copy).then_inc(ws_c, 1)
            with act.Fori(1, 4) as i:
                for j in range(2):
                    for tg in range(3):
                        act.wait_ge(full[tg], 2 * i + j + 1)
                        fn(uv[:, 2 * i + j, tgc[tg]], bank[tg][:, 0:TG], ACT.Copy).then_inc(free[tg], 1)
                    split_in(0, 2, i, j, 2 * i + j + 1)

            def qkv_copy(pair, j, tg):
                act.wait_ge(full[tg], M0[f"qkv{pair}"] + j + 1)
                src = bank[tg][:, 0:TG]
                n = TG // 4 if tg < 2 else (SEQ - 2 * TG) // 4
                if j < 6:
                    out = qk[:, j, 0:SEQ].rearrange("p (r i) -> p r i", r=4)[:, :, TG // 4 * tg:TG // 4 * tg + n]
                    a = fn(out, src[:, 0:4 * n].rearrange("p (i r) -> p r i", r=4), ACT.Copy)
                else:
                    a = fn(vT[:, j - 6, TG * tg:TG * tg + 4 * n], src[:, 0:4 * n], ACT.Copy)
                if tg == 2:
                    a.then_inc(act_s, 1)
                    a = fn(sqkv[:, pair, j, :], src[:, 4 * n:TG], ACT.Copy)
                    act.wait_ge(act_s, 9 * pair + j + 1)
                a.then_inc(free[tg], 1)

            def kv_copy(pair):
                for a in range(0, 11, 2):
                    act.wait_ge(kv_t, 11 * pair + a + 1)
                    n = 1 if a == 6 else 4
                    out = vtok[:, 4 * a:4 * a + n] if a < 7 else kst[:, 4 * (a - 7):4 * (a - 7) + 4]
                    fn(out, by4(psK[a % 4])[:, 0:n], ACT.Copy).then_inc(kv_c[0], 1)

            def gelus(c):
                n = P if c < 8 else NS
                cols = slice(P * c, P * c + n)
                if c:
                    act.wait_ge(ln_t, c)
                fn(vc[:, :, 0:n], uv[:, 4:8, cols], ACT.Gelu_apprx_tanh).then_inc(ln_v, 1)
                fn(uv[:, 0:4, cols], uv[:, 0:4, cols], ACT.Gelu_apprx_tanh).then_inc(ln_u, 1)

            for tg in range(3):
                act.wait_ge(free[tg], M0["qkv0"] + 1)
            gelus(0)
            for j in range(9):
                n = P if j < 8 else NS
                rows = n
                qkv_copy(0, j, 0)
                act.wait_ge(ln_var, j + 1)
                fn(stat[0:rows, 40:41], stat[0:rows, 39:40], ACT.Sqrt).then_inc(ln_sd, 1)
                qkv_copy(0, j, 1)
                if j < 8:
                    gelus(j + 1)
                qkv_copy(0, j, 2)
                act.wait_ge(ln_o, j + 1)
                fn(ob_hi[:, :, P * j:P * j + n], mixt[:, :, 0:n], ACT.Copy).then_inc(ln_hi, 1)
                split_in(U0["qkv0"], 0, 0, j, M0["qkv0"] + j + 1)
            kv_copy(0)

            act.wait_ge(sgv_out, 16)
            with act.Fori(0, 2) as i:
                for j in range(2):
                    for b in range(2):
                        for tg in range(3):
                            m = 4 * i + 2 * j + b
                            act.wait_ge(full[tg], M0["pb"] + m + 1)
                            fn(mb[:, m, tgc[tg]], bank[tg][:, 0:TG], ACT.Copy, scale=0.5).then_inc(free[tg], 1)
                    split_in(U0["pb"], 2, i, j, M0["pb"] + 4 * i + 2 * j + 2)

            def attention(pair, U, M):
                def probs(i, n):
                    N, w = 16 * pair + 8 * i + n, 1152 if n // 2 % 2 else 768
                    act.wait_ge(at_m, N + 2)
                    fn(pr[:, n % 2, 0:w], pr[:, n % 2, 0:w], ACT.Exp, scale=SCALE, bias=stat[:, 48 + n % 2:49 + n % 2],
                       accum_out=stat[:, 50 + n % 2:51 + n % 2]).then_inc(at_p, 1)

                def copy0(i, n):
                    N = 16 * pair + 8 * i + n
                    act.wait_ge(at_t0, N + 1)
                    act.wait_ge(at_pv, N + 1)
                    fn(prT[:, 0:4, :], by4(psT[0]), ACT.Copy).then_inc(at_c0, 1)

                def ocopy(i, t):
                    T = 8 * pair + 4 * i + t
                    act.wait_ge(at_ot, T + 3)
                    out = oaT[:, pair, 0:SEQ].rearrange("p (h i r) -> p h r i", h=2, r=4)
                    fn(out[:, t % 2, bass.ds(2 * i + t // 2, 1), :].rearrange("p o i -> p (o i)"), psO[:, 384:512],
                       ACT.Copy).then_inc(at_oc, 1)

                def gate(i, q):
                    m, G = M + 2 * i + q // 3, 12 * pair + 6 * i + q
                    act.wait_ge(full[q % 3], m + 1)
                    act.wait_ge(at_gu, G + 1)
                    fn(gt[:, q % 2, :], gbank[q % 2][:, 0:TG], ACT.Tanh, scale=0.5).then_inc(free[q % 3], 1)
                    if q % 3 == 2:
                        split_in(U, 2, i, q // 3, m + 1)

                with act.Fori(0, 2) as i:
                    probs(i, 0)
                    gate(i, 0)
                    for n in range(1, 9):
                        if n in (3, 5, 7):
                            ocopy(i, (n - 3) // 2)
                        copy0(i, n - 1)
                        if n < 8:
                            probs(i, n)
                        for q in gates_done(n):
                            gate(i, q)
                    ocopy(i, 3)

            attention(0, U0["gb0"], M0["gb0"])
            for j in range(9):
                if j == 6:
                    act.wait_ge(kv_d, 16 * 32)
                for tg in range(3):
                    qkv_copy(1, j, tg)
                split_in(U0["qkv1"], 0, 0, j, M0["qkv1"] + j + 1)
            kv_copy(1)
            attention(1, U0["gb1"], M0["gb1"])

            def oa_high(tg):
                act.wait_ge(full[tg], M0["pa"])
                fn(oa_hi[:, :, tgc[tg]], oaT[:, :, tgc[tg]], ACT.Copy).then_inc(oa_h, 1)

            act.wait_ge(kv_d, 16 * 64)
            for j in range(8):
                for tg in range(3):
                    act.wait_ge(full[tg], M0["ga"] + j + 1)
                    fn(ga[:, j, tgc[tg]], bank[tg][:, 0:TG], ACT.Tanh, scale=0.5).then_inc(free[tg], 1)
                    if j == 5 and tg == 1:
                        act.wait_ge(s_ssr, 1)
                        fn(ssr[:, 0:312], ssr[:, 0:312], ACT.Exp, scale=SCALE, bias=stat[0:32, 53:54],
                           accum_out=stat[0:32, 54:55]).then_inc(s_exp, 1)
                    if j == 7 and tg:
                        oa_high(tg - 1)
                if j < 7:
                    split_in(U0["ga"], 0, 0, j, M0["ga"] + j + 1)
            act.wait_ge(s_oa, 2)
            oa_high(2)
            split_in(U0["ga"], 0, 0, 7, M0["ga"] + 8)

            for k in range(24):
                act.wait_ge(m_t, k + 1)
                fn(m_hi[:, k // 3, tgc[k % 3]], pt[:, 2 * (k % 2) + 1, :], ACT.Copy).then_inc(m_h, 1)
                if k % 12 == 11:
                    split_in(U0["pa"], 0, 0, k // 12, M0["pa"] + 4 * (k // 12) + 4)

            def x_copy(t):
                n = P if t < 8 else NS
                act.wait_ge(xr_t, t + 1)
                fn(xT[:, 0:4, P * t:P * t + n], by4(psT[0], n), ACT.Copy).then_inc(xr_c[0], 1)

            def y1_copy(j, tg, src):
                act.wait_ge(full[tg], M0["wo"] + j + 1)
                fn(y1[:, j, tgc[tg]], src[:, 0:TG], ACT.Copy).then_inc(free[tg], 1)

            for j in range(WT):
                for tg in range(3):
                    y1_copy(j, tg, bank[tg])
                    if (j, tg) in X_TURNS:
                        x_copy(X_TURNS.index((j, tg)))
                split_in(U0["wo"], 0, 0, j, M0["wo"] + j + 1)

            def root(phase, tg):
                act.wait_ge(n_v[phase], tg + 1)
                fn(stat[:, 9 * phase + 3:9 * phase + 6], stat[:, 9 * phase:9 * phase + 3], ACT.Sqrt).then_inc(n_sd[phase], 1)

            def squares(tg, ms):
                for m in ms:
                    k = 8 * tg + m
                    act.wait_ge(x1_s, k + 1)
                    fn(nt_[:, k % 3, :], xT[:, m, tgc[tg]], ACT.Square).then_inc(x1_q, 1)
                    fn(f_hi[:, m, tgc[tg]], xT[:, m, tgc[tg]], ACT.Copy, scale=gains[:, 1, m:m + 1]).then_inc(f_h, 1)

            def y1_pair(n):
                y1_copy(WT + n % 2, n // 2, bank[n % 3])

            def r2_copy(tg):
                act.wait_ge(n_b[1], tg + 1)
                fn(r2[:, tg, :], psT[1][:, 0:TG], ACT.Copy).then_inc(r2_s, 1)

            def silu(m, tg):
                act.wait_ge(free[tg], m + 2)
                fn(sg[:, tgc[tg]], sg[:, tgc[tg]], ACT.Silu).then_inc(ff_sg, 1)

            def a_high(m, j, tg):
                act.wait_ge(free[tg], m + 2)
                fn(a_hi[:, j, tgc[tg]], sq[:, (3 * j + tg) % 2, :], ACT.Copy).then_inc(ff_h, 1)

            for n in range(3):
                y1_pair(n)
            root(0, 0)
            y1_pair(3)
            squares(0, range(0, 3))
            y1_pair(4)
            split_in(U0["wo"], 0, 0, 6, M0["wo"] + 7)
            squares(0, range(3, 7))
            y1_pair(5)
            split_in(U0["wo"], 0, 0, 7, M0["wo"] + 8)
            squares(0, range(7, 8))
            for tg in range(3):
                if tg < 2:
                    root(0, tg + 1)
                root(1, tg)
                r2_copy(tg)
                m = M0["ffn"]
                if tg < 2:
                    squares(tg + 1, range(0, 3))
                silu(m, tg)
                if tg < 2:
                    squares(tg + 1, range(3, 8))
                else:
                    split_in(U0["ffn"], 0, 0, 0, M0["ffn"] + 1)
                a_high(m + 1, 0, tg)
            split_in(U0["ffn"], 0, 0, 1, M0["ffn"] + 2)

            def ffn_round(i):
                for j in range(1 if isinstance(i, int) else 0, FG):
                    m = M0["ffn"] + 16 * i + 2 * j
                    for tg in range(3):
                        silu(m, tg)
                    split_in(U0["ffn"], 12, i, 2 * j, m + 1)
                    for tg in range(3):
                        a_high(m + 1, j, tg)
                    split_in(U0["ffn"], 12, i, 2 * j + 1, m + 2)
                for j in range(4):
                    split_in(U0["ffn"], 12, i, 8 + j, M0["ffn"] + 16 * i + 8 + 2 * j + 2)
            ffn_round(0)
            with act.Fori(1, ROUNDS) as i:
                ffn_round(i)
            for j in range(2):
                m = M0["tail"] + 2 * j
                for tg in range(3):
                    silu(m, tg)
                split_in(U0["tail"], 0, 0, 2 * j, m + 1)
                for tg in range(3):
                    a_high(m + 1, j, tg)
                split_in(U0["tail"], 0, 0, 2 * j + 1, m + 2)
            act.wait_ge(ff_l, 3 * KF + 2)
            for k in range(24):
                tg, b = k // 8, k % 8
                act.wait_ge(free[tg], M0["tail"] + 4 + b + 2)
                if k >= 2:
                    act.wait_ge(y2_a, k - 1)
                fn(sq[:, k % 2, :], y2[:, b, tgc[tg]], ACT.Square).then_inc(y2_q, 1)
                if k in (13, 21):
                    root(2, 0 if k == 13 else 1)
            root(2, 2)
            for q, t in enumerate(Z_ORDER):
                dst, rows = (yt[:, t, :], P) if t < 8 else (yts[:], NS)
                act.wait_ge(z_turn, q + 1)
                for a in range(2 if q < 5 else 1):
                    fn(dst[:, 512 * a:512 * a + 512], psZ[q][a][0:rows, :], ACT.Copy).then_inc(z_c[0], 1)

        @block.vector
        def _(dve):
            v = nc.vector
            st = Steps(dve, dve_s)
            for tg in range(3):
                dve.sem_inc(free[tg], 1)
            dve.sem_inc(at_m, 1)
            dve.sem_inc(at_c1, 1)
            dve.sem_inc(at_o, 1)
            dve.sem_inc(at_gu, 2)

            def lo_split(u, par):
                dve.wait_ge(w_hi_s, u + 1)
                v.tensor_tensor(w_lo[par][:], w_raw[par][:], w_hi[par][:].bitcast(F32), ALU.subtract).then_inc(w_lo_s, 1)

            def lo_in(u0, per, i, j):
                par = (u0 + j) % 2
                u = u0 + j + 2 + per * i
                if not isinstance(u, int) or u < UNITS:
                    lo_split(u, par)

            def x_low(t):
                n = P if t < 8 else NS
                for a in range(2):
                    dve.wait_ge(x_hi, 2 * t + a + 1)
                    hi = h_hi[:, 4 * a:4 * a + 4, P * t:P * t + n].bitcast(F32)
                    ins = v.tensor_tensor(h_lo[:, 4 * a:4 * a + 4, P * t:P * t + n], by4(psX[t % 2][a], n), hi, ALU.subtract)
                    if a == 0:
                        st.link(ins)
                ins.then_inc(x_lo, 1)

            def mean_square(t):
                rows = P if t < 8 else NS
                dve.wait_ge(x_sq, t + 1)
                v.tensor_scalar(stat[0:rows, 9 + t:10 + t], stat[0:rows, t:t + 1], 1.0 / D, EPS, ALU.mult, ALU.add
                                ).then_inc(x_v, 1)

            mean_square(0)
            for t in range(9):
                src, rows = (xin[t], P) if t < 8 else (xins, NS)
                dve.wait_ge(x_sd, t + 1)
                st.link(v.reciprocal(stat[0:rows, 27 + t:28 + t], stat[0:rows, 18 + t:19 + t]))
                if t < 8:
                    mean_square(t + 1)
                dve.wait_ge(x_g, t + 1)
                v.tensor_scalar(src[0:rows, :], src[0:rows, :], stat[0:rows, 27 + t:28 + t], None, ALU.mult).then_inc(x_h, 1)
                if t:
                    x_low(t - 1)
                if t in (2, 3):
                    lo_split(t - 2, t - 2)
            x_low(8)
            dve.wait_ge(iota_s, 1)
            st.link(v.tensor_single_scalar(iom[:], iot[:], 3, ALU.bitwise_and))
            v.tensor_scalar(m_far[:, 1, :], iom[:], 0.0, NEG, ALU.is_gt, ALU.mult).then_inc(far_s, 1)

            with dve.Fori(0, 4) as i:
                for j in range(2):
                    lo_in(0, 2, i, j)

            def kv_copy(pair):
                if pair:
                    dve.wait_ge(kv_d, 16 * 32)
                for a in range(1, 11, 2):
                    dve.wait_ge(kv_t, 11 * pair + a + 1)
                    out = vtok[:, 4 * a:4 * a + 4] if a < 7 else kst[:, 4 * (a - 7):4 * (a - 7) + 4]
                    v.tensor_copy(out, by4(psK[a % 4])).then_inc(kv_c[1], 1)

            dve.wait_ge(small_in, 96)
            for c in range(9):
                n = P if c < 8 else NS
                dve.wait_ge(ln_t, c + 1)
                st.link(v.bn_stats(stat[0:n, 30:36], psT[0][0:n, :]))
                st.link(v.bn_aggr(stat[0:n, 36:38], stat[0:n, 30:36]))
                v.tensor_scalar(stat[0:n, 39:40], stat[0:n, 37:38], EPS, None, ALU.add).then_inc(ln_var, 1)
                dve.wait_ge(ln_sd, c + 1)
                st.link(v.reciprocal(stat[0:n, 41:42], stat[0:n, 40:41]))
                if c:
                    dve.wait_ge(ln_mix, c)
                st.link(v.tensor_scalar(vt[0:n, :], psT[0][0:n, :], stat[0:n, 36:37], stat[0:n, 41:42], ALU.subtract, ALU.mult))
                st.link(v.tensor_tensor(vt[0:n, :], vt[0:n, :], lnvg[0:n, :], ALU.mult))
                v.tensor_tensor(vt[0:n, :], vt[0:n, :], lnvb[0:n, :], ALU.add).then_inc(ln_n, 1)
                dve.wait_ge(ln_n, c + 1)
                if c == 8:
                    for g in range(4):
                        st.link(v.tensor_scalar(vw[:, P * g:P * g + P], vt[0:NS, P * g:P * g + P], w00[:, g:g + 1],
                                                w00[:, 4 + g:5 + g], ALU.mult, ALU.add))
                    dve.sem_inc(ln_w, 1)
                dve.wait_ge(ln_mix, c + 1)
                dve.wait_ge(ln_u, c + 1)
                cols = slice(P * c, P * c + n)
                if c < 8:
                    st.link(v.tensor_tensor(mixt[:], by4(psA), bsg[:], ALU.add))
                    v.tensor_tensor(mixt[:], mixt[:], uv[:, 0:4, cols], ALU.mult).then_inc(ln_o, 1)
                else:
                    v.tensor_tensor(mixt[:, :, 0:n], by4(psA, n), uv[:, 0:4, cols], ALU.mult).then_inc(ln_o, 1)
                dve.wait_ge(ln_hi, c + 1)
                v.tensor_tensor(ob_lo[:, :, cols], mixt[:, :, 0:n], ob_hi[:, :, cols].bitcast(F32), ALU.subtract
                                ).then_inc(ln_lo, 1)
                dve.wait_ge(ln_lo, c + 1)
                lo_in(U0["qkv0"], 0, 0, c)
            kv_copy(0)
            with dve.Fori(0, 2) as i:
                for j in range(2):
                    lo_in(U0["pb"], 2, i, j)

            dve.wait_ge(masks_s, 1)

            def attention(pair, U, M):
                def maxima(i, n):
                    r, hh = 2 * i + n // 4, n // 2 % 2
                    N, s_ = 16 * pair + 8 * i + n, n % 2
                    mx = [stat[:, 42 + 3 * s_ + a:43 + 3 * s_ + a] for a in range(3)]
                    w = P * (hh + 1)
                    dve.wait_ge(at_s, N + 4)
                    dve.wait_ge(at_t1, N + 1)
                    if n % 4 == 0:
                        st.link(v.tensor_copy(m_now[:], m_main[:, bass.ds(3 - r, 4), :]))
                        st.link(v.tensor_copy(e_now[:], m_edge[:, :, bass.ds(3 - r, 4)]))

                    v.memset(stat[:, 63:64], 0.0)

                    def add_max(out, in0, in1, accum):
                        return v.tensor_tensor_reduce(out, in0, in1, 1.0, NEG, ALU.add, ALU.max, accum)

                    far = add_max(pr[:, s_, 512:512 + 2 * w].rearrange("p (g i) -> p g i", g=2),
                                  psB[:, 0:2 * w].rearrange("p (g i) -> p g i", g=2), m_far[:, :, 256 - w:256], mx[1])
                    st.mark(far)
                    if hh:
                        st.mark(add_max(pr[:, s_, 1024:1152].rearrange("p (i c) -> p i c", c=4),
                                        psC[:, 0:P].rearrange("p (i c) -> p i c", c=4), e_now[:], mx[2]))
                    st.link(add_max(pr[:, s_, 0:512].rearrange("p (c i) -> p c i", c=4),
                                    psA[:, :].rearrange("p (c i) -> p c i", c=4), m_now[:], mx[0]))
                    if hh:
                        st.link(v.tensor_scalar(mx[0], mx[0], mx[2], None, ALU.max))
                    v.tensor_scalar(stat[:, 48 + s_:49 + s_], mx[0], mx[1], -SCALE, ALU.max, ALU.mult).then_inc(at_m, 1)

                def copy1(i, n):
                    N, hh = 16 * pair + 8 * i + n, n // 2 % 2
                    dve.wait_ge(at_t1, N + 3)
                    dve.wait_ge(at_pv, N + 1)
                    ins = v.tensor_copy(prT[:, 4:8 if hh else 6, :], by4(psT[1])[:, 0:4 if hh else 2])
                    if hh:
                        st.link(ins)
                        ins = v.tensor_copy(prT[:, 8, :], psO[:, 256:384])
                    ins.then_inc(at_c1, 1)

                def gated(i, q):
                    G = 12 * pair + 6 * i + q
                    part = mb[:, bass.ds(4 * pair + 2 * i + q // 3, 1), tgc[q % 3]].rearrange("p o t -> p (o t)")
                    dve.wait_ge(free[q % 3], M + 2 * i + q // 3 + 2)
                    v.scalar_tensor_tensor(part, gt[:, q % 2, :], 1.0, part, ALU.add, ALU.mult).then_inc(at_gu, 1)

                def outputs(i, n):
                    N, T = 16 * pair + 8 * i + n, 8 * pair + 4 * i + n // 2
                    e = n % 2
                    dve.wait_ge(at_pv, N + 2)
                    dve.wait_ge(at_ot, T + 1)
                    st.link(v.reciprocal(stat[:, 52:53], stat[:, 50 + e:51 + e]))
                    v.tensor_scalar(otok[:, n // 2 % 2, HD * e:HD * e + HD], psO[:, P:P + HD], stat[:, 52:53], None, ALU.mult
                                    ).then_inc(at_o, 1)

                with dve.Fori(0, 2) as i:
                    st.enter(i, 4 * 2 + 4 * 4 + 4 + 4 + 8)
                    maxima(i, 0)
                    gated(i, 0)
                    for n in range(1, 9):
                        copy1(i, n - 1)
                        if n < 8:
                            maxima(i, n)
                        for q in gates_done(n):
                            gated(i, q)
                        outputs(i, n - 1)
                        if 2 in gates_done(n):
                            lo_in(U, 2, i, 0)
                        if 5 in gates_done(n):
                            lo_in(U, 2, i, 1)
                st.leave(2)

            attention(0, U0["gb0"], M0["gb0"])
            for j in range(9):
                lo_in(U0["qkv1"], 0, 0, j)
            kv_copy(1)
            attention(1, U0["gb1"], M0["gb1"])

            dve.wait_ge(kv_d, 16 * 64)
            dve.wait_ge(at_oc, 17)
            st.link(v.memset(qz[:], 0.0))
            for p in range(2):
                for e in range(2):
                    hd = slice(HD * e, HD * e + HD)
                    st.link(v.tensor_copy(qz[hd, p, :, :, e], sqkv[hd, p, 0:3, :]))
            dve.sem_inc(s_qz, 1)
            dve.wait_ge(s_nt, 1)
            for g in range(GROUPS):
                v.tensor_copy(svt[:, g].rearrange("b k c -> b (k c)"), [psA, psB, psC][g][0:NS, :]).then_inc(s_nc, 1)
            v.tensor_copy(qtok[:, 0:2, :].rearrange("b g c -> b (g c)"), psT[0][0:NS, :]).then_inc(s_nc, 1)
            v.tensor_copy(qtok[:, 2, :], psT[1][0:NS, 0:256]).then_inc(s_nc, 1)

            def oa_low(tg):
                dve.wait_ge(oa_h, tg + 1)
                v.tensor_tensor(oa_lo[:, :, tgc[tg]], oaT[:, :, tgc[tg]], oa_hi[:, :, tgc[tg]].bitcast(F32), ALU.subtract
                                ).then_inc(oa_s, 1)

            def k_scores(kk):
                n, g = kk // 3, kk % 3
                ck = CKEYS[g]
                dve.wait_ge(sk_in[kk % 2], 16 * (kk // 2 + 1))
                dve.wait_ge(sq_in[kk % 2], 16 * (kk // 2 + 1))
                if kk >= 2:
                    dve.wait_ge(s_sc, kk - 1)
                v.tensor_tensor(kq[0:ck, kk % 2, :], kraw[0:ck, kk % 2, :], qb[0:ck, kk % 2, :], ALU.mult).then_inc(s_kq, 1)
                dve.wait_ge(s_kq, kk + 1)
                v.tensor_reduce(sst[0:ck, 0, 32 * g + 4 * n:32 * g + 4 * n + 4],
                                kq[0:ck, kk % 2, :].rearrange("p (s d) -> p s d", d=HD), mybir.AxisListType.X, ALU.add
                                ).then_inc(s_sc, 1)

            for j in range(8):
                for kk in range(5 * j, min(5 * j + 5, 24)):
                    k_scores(kk)
                if j == 5:
                    dve.wait_ge(s_self, 1)
                    v.tensor_copy(sst[0:NS, 1, :], psB[0:NS, 0:96]).then_inc(s_sst, 1)
                    dve.wait_ge(s_rows, 1)
                    dve.wait_ge(masks_s, 2)
                    st.link(v.tensor_copy(ssr[:, 0:288], psC[0:32, 0:288]))
                    st.link(v.tensor_tensor(ssr[:, 288:312], psC[0:32, 288:312], smask[:].rearrange("p g n -> p (g n)"), ALU.add))
                    st.link(v.reduce_max(stat[0:32, 55:56], ssr[:, 0:312], mybir.AxisListType.X))
                    v.tensor_scalar(stat[0:32, 53:54], stat[0:32, 55:56], -SCALE, None, ALU.mult).then_inc(s_ssr, 1)
                    dve.wait_ge(s_exp, 1)
                    st.link(v.reciprocal(stat[0:32, 56:57], stat[0:32, 54:55]))
                    v.tensor_scalar(ssr[:, 0:312], ssr[:, 0:312], stat[0:32, 56:57], None, ALU.mult).then_inc(s_pn, 1)
                if j == 6:
                    dve.wait_ge(s_pt, 1)
                    v.tensor_copy(spT[:, 0:2, :].rearrange("p g n -> p (g n)"), psA[:, 0:64]).then_inc(s_ptc, 1)
                    v.tensor_copy(spT[0:32, 2, :], psA[0:32, 64:96]).then_inc(s_ptc, 1)
                    v.tensor_copy(spT[0:NS, 3:6, :].rearrange("p g n -> p (g n)"), psA[0:NS, 96:192]).then_inc(s_ptc, 1)
                if j == 7:
                    oa_low(0)
                else:
                    lo_in(U0["ga"], 0, 0, j)
            dve.wait_ge(s_pv, 1)
            for e in range(2):
                hd = slice(HD * e, HD * e + HD)
                v.tensor_copy(oaT[hd, :, SEQ:NT], psB[hd, 0:32].rearrange("d (p n e) -> d p n e", p=2, e=2)[:, :, :, e]
                              ).then_inc(s_oa, 1)

            oa_low(1)
            oa_low(2)
            lo_in(U0["ga"], 0, 0, 7)

            def merge_product(k):
                m, tg = k // 3, k % 3
                dve.wait_ge(full[tg], M0["pa"] + m + 1)
                if k >= 2:
                    dve.wait_ge(m_t, k - 1)
                v.scalar_tensor_tensor(pt[:, 2 * (k % 2), :], ga[:, m, tgc[tg]], 1.0, bank[tg][:, 0:TG], ALU.add, ALU.mult
                                       ).then_inc(free[tg], 1)

            merge_product(0)
            for k in range(24):
                m, tg = k // 3, k % 3
                if k < 23:
                    merge_product(k + 1)
                dve.wait_ge(free[tg], M0["pa"] + m + 2)
                if k >= 2:
                    dve.wait_ge(m_l, k - 1)
                v.scalar_tensor_tensor(pt[:, 2 * (k % 2) + 1, :], pt[:, 2 * (k % 2), :], 0.5, mb[:, m, tgc[tg]], ALU.mult, ALU.add
                                       ).then_inc(m_t, 1)
                if k in (14, 23):
                    lo_in(U0["pa"], 0, 0, k // 15)

            def x_copy(t):
                n = P if t < 8 else NS
                dve.wait_ge(xr_t, t + 1)
                v.tensor_copy(xT[:, 4:8, P * t:P * t + n], by4(psT[1], n)).then_inc(xr_c[1], 1)

            dve.wait_ge(gains_s, 1)
            for j in range(WT):
                for tg in range(3):
                    if (j, tg) in X_TURNS:
                        x_copy(X_TURNS.index((j, tg)))
                lo_in(U0["wo"], 0, 0, j)

            cols = [(stat[:, 9 * ph:9 * ph + 3], stat[:, 9 * ph + 3:9 * ph + 6], stat[:, 9 * ph + 6:9 * ph + 9]) for ph in range(3)]
            r2c = [stat[:, 30 + 3 * tg:33 + 3 * tg] for tg in range(3)]

            def head(phase, tg):
                ps = (psT[0] if phase == 0 else psC)[:, 0:3]
                var = cols[phase][0]
                dve.wait_ge(n_s[phase], tg + 1)
                if phase == 2:
                    st.link(v.tensor_tensor(var, ps, r2c[tg], ALU.mult))
                    st.link(v.tensor_tensor(var, var, r2c[tg], ALU.mult))
                    ps = var
                v.tensor_scalar(var, ps, 1.0 / D, EPS, ALU.mult, ALU.add).then_inc(n_v[phase], 1)

            def tail(phase, tg):
                r = r2c[tg] if phase == 1 else cols[phase][2]
                dve.wait_ge(n_sd[phase], tg + 1)
                if tg:
                    dve.wait_ge(n_b[phase], tg)
                elif phase == 2:
                    dve.wait_ge(n_b[0], 3)
                st.link(v.reciprocal(r, cols[phase][1]))
                if phase == 2:
                    st.link(v.tensor_tensor(r, r, r2c[tg], ALU.mult))
                for j in range(3):
                    ins = v.tensor_scalar((diag2 if phase == 1 else diag)[:, j, :], ident[:], r[:, j:j + 1], None, ALU.mult)
                ins.then_inc(n_d[phase], 1)

            def apply(tg, at_step={}):
                dve.wait_ge(n_b[0], tg + 1)
                for m in range(KD + 2):
                    k = 8 * tg + m
                    if m < KD:
                        if k >= 3:
                            dve.wait_ge(x1_a, k - 2)
                        v.scalar_tensor_tensor(nt_[:, k % 3, :], y1[:, m, tgc[tg]], gains[:, 0, m:m + 1],
                                               psR[tg % 2][:, 0:TG], ALU.mult, ALU.mult).then_inc(x1_t, 1)
                    if m in at_step:
                        at_step[m]()
                    if m >= 2:
                        k, n = k - 2, m - 2
                        dve.wait_ge(x1_q, k + 1)
                        if n == 0:
                            v.tensor_copy(acc[:, tg, :], nt_[:, k % 3, :]).then_inc(x1_a, 1)
                        else:
                            dve.wait_ge(x1_a, k)
                            v.tensor_tensor(acc[:, tg, :], acc[:, tg, :], nt_[:, k % 3, :], ALU.add).then_inc(x1_a, 1)
                        dve.wait_ge(f_h, k + 1)
                        v.scalar_tensor_tensor(f_lo[:, n, tgc[tg]], xT[:, n, tgc[tg]], gains[:, 1, n:n + 1],
                                               f_hi[:, n, tgc[tg]].bitcast(F32), ALU.mult, ALU.subtract).then_inc(f_l, 1)

            def gate(m, tg, src):
                dve.wait_ge(full[tg], m + 1)
                v.tensor_tensor(sg[:, tgc[tg]], src[:, 0:TG], r2[:, tg, :], ALU.mult).then_inc(free[tg], 1)

            def product(m, j, tg, g3, src):
                dve.wait_ge(full[tg], m + 1)
                dve.wait_ge(ff_sg, g3 + 1)
                dve.wait_ge(ff_l, g3 + 1)
                v.tensor_tensor(sq[:, (3 * j + tg) % 2, :], src[:, 0:TG], sg[:, tgc[tg]], ALU.mult).then_inc(free[tg], 1)

            def y2_add(m, c, tg, src, first=False):
                dve.wait_ge(full[tg], m + 1)
                part = y2[:, c, tgc[tg]]
                if first:
                    v.tensor_copy(part, src[:, 0:TG]).then_inc(free[tg], 1)
                else:
                    v.tensor_tensor(part, part, src[:, 0:TG], ALU.add).then_inc(free[tg], 1)

            head(0, 0)
            tail(0, 0)
            apply(0, {6: lambda: lo_in(U0["wo"], 0, 0, 6)})
            lo_in(U0["wo"], 0, 0, 7)
            for tg in range(3):
                if tg < 2:
                    head(0, tg + 1)
                head(1, tg)
                if tg < 2:
                    tail(0, tg + 1)
                tail(1, tg)

                def gate_first(tg=tg):
                    dve.wait_ge(r2_s, tg + 1)
                    gate(M0["ffn"], tg, bank[2 * tg % 3])
                if tg < 2:
                    apply(tg + 1, {5: gate_first})
                else:
                    gate_first()
                    lo_in(U0["ffn"], 0, 0, 0)
                product(M0["ffn"] + 1, 0, tg, tg, bank[(2 * tg + 1) % 3])
            lo_in(U0["ffn"], 0, 0, 1)

            def ffn_round(i):
                first = isinstance(i, int)
                for j in range(1 if first else 0, FG):
                    for tg in range(3):
                        gate(M0["ffn"] + 16 * i + 2 * j, tg, bank[tg])
                    lo_in(U0["ffn"], 12, i, 2 * j)
                    for tg in range(3):
                        product(M0["ffn"] + 16 * i + 2 * j + 1, j, tg, 12 * i + 3 * j + tg, bank[tg])
                    lo_in(U0["ffn"], 12, i, 2 * j + 1)
                for j in range(4):
                    for b in range(2):
                        for tg in range(3):
                            y2_add(M0["ffn"] + 16 * i + 8 + 2 * j + b, 2 * j + b, tg, bank[tg], first)
                    lo_in(U0["ffn"], 12, i, 8 + j)
            ffn_round(0)
            with dve.Fori(1, ROUNDS) as i:
                ffn_round(i)
            for j in range(2):
                for tg in range(3):
                    gate(M0["tail"] + 2 * j, tg, bank[tg])
                lo_in(U0["tail"], 0, 0, 2 * j)
                for tg in range(3):
                    product(M0["tail"] + 2 * j + 1, j, tg, 12 * ROUNDS + 3 * j + tg, bank[tg])
                lo_in(U0["tail"], 0, 0, 2 * j + 1)

            def z_term(tg, m):
                dve.wait_ge(n_b[2], tg + 1)
                part = y2[:, m, tgc[tg]]
                v.scalar_tensor_tensor(part, part, gains[:, 2, m:m + 1], psR[tg % 2][:, 0:TG], ALU.mult, ALU.mult
                                       ).then_inc(z_t, 1)

            def z_add(tg, m):
                dve.wait_ge(z_t, 8 * tg + m + 1)
                part = xT[:, m, tgc[tg]]
                v.tensor_tensor(part, part, y2[:, m, tgc[tg]], ALU.add).then_inc(z_s[0], 1)

            for n in range(24):
                tg, b = n // 8, n % 8
                if n in (13, 21):
                    head(2, n // 8 - 1)
                y2_add(M0["tail"] + 4 + b, b, tg, bank[n % 3])
                if n in (14, 22):
                    tail(2, n // 8 - 1)
                if n >= 16:
                    z_term(0, b)
            for m in range(5):
                z_term(1, m)
            head(2, 2)
            for m in range(5, 8):
                z_term(1, m)
            tail(2, 2)
            for m in range(8):
                z_add(1, m)
            for m in range(8):
                z_term(2, m)
                if 1 <= m < 7:
                    z_add(2, m - 1)
            for q in range(5, 9):
                t = Z_ORDER[q]
                dst, rows = (yt[:, t, :], P) if t < 8 else (yts[:], NS)
                dve.wait_ge(z_turn, q + 1)
                v.tensor_copy(dst[:, 512:D], psZ[q][1][0:rows, :]).then_inc(z_c[1], 1)

        @block.gpsimd
        def _(pool):
            g_ = nc.gpsimd
            st = Steps(pool, pool_s)
            pool.sem_inc(ff_l, 2)
            st.link(g_.memset(ident[:], 0.0))
            g_.affine_select(out=ident[:], in_=ident[:], compare_op=ALU.not_equal, fill=1.0, base=0, pattern=[[-1, P]],
                             channel_multiplier=1).then_inc(ident_s, 1)
            pool.wait_ge(gpre_in, 16)
            for t in range(9):
                src, rows = (xin[t], P) if t < 8 else (xins, NS)
                pool.wait_ge(x_sq, t + 1)
                g_.tensor_tensor(src[0:rows, :], src[0:rows, :], g_pre[0:rows, :], ALU.mult).then_inc(x_g, 1)
            pool.wait_ge(small_in, 96)
            for g in range(4):
                g_.affine_select(out=wsg[:, g, :], in_=wsg[:, g, :], compare_op=ALU.is_ge, fill=0.0, base=0,
                                 pattern=[[-1, P]], channel_multiplier=1).then_inc(tril_s, 1)

            def keep(t, base_, pattern, mult):
                return g_.affine_select(out=t, in_=t, compare_op=ALU.is_ge, fill=NEG, base=base_, pattern=pattern,
                                        channel_multiplier=mult)
            g_.iota(iot[:], pattern=[[-1, 256]], base=P, channel_multiplier=1).then_inc(iota_s, 1)
            st.link(g_.memset(ones[:], 1.0))
            st.link(g_.memset(m_main[:], 0.0))
            st.link(keep(m_main[:], 3, [[-1, 7], [-4, P]], 4))
            st.link(keep(m_main[:], 125, [[1, 7], [4, P]], -4))
            st.link(g_.memset(m_edge[:], 0.0))
            st.link(keep(m_edge[:], -3, [[4, 32], [1, 7]], -4))
            st.link(g_.memset(m_far[:, 0, :], 0.0))
            st.link(keep(m_far[:, 0, :], P, [[-1, 256]], 1))
            st.link(keep(m_far[:, 0, :], 0, [[1, 256]], -1))
            pool.wait_ge(far_s, 1)
            keep(m_far[:, 1, :], P, [[-1, 256]], 1).then_inc(masks_s, 1)

            def queries(pair):
                qst = (qst0, qst1)[pair]

                def tile(i, t):
                    T = 8 * pair + 4 * i + t
                    pool.wait_ge(at_s, 2 * T + 1)
                    for e in range(2):
                        hd = slice(HD * e, HD * e + HD)
                        g_.tensor_copy(qst[hd, t % 2, e], qk[hd, 0:3, bass.ds(256 * (2 * i + t // 2) + P * (t % 2), P)]
                                       ).then_inc(at_q, 1)
                with pool.Fori(0, 2) as i:
                    for t in range(4):
                        tile(i, t)

            for pair in range(2):
                if pair == 0:
                    pool.wait_ge(kv_d, 16 * 32)
                else:
                    pool.wait_ge(full[2], M0["gb0"])
                    pool.wait_ge(at_q, 16)
                st.link(g_.memset((qst0, qst1)[pair][:], 0.0))
                for tg in range(3):
                    pool.wait_ge(free[tg], M0[f"qkv{pair}"] + 10)
                queries(pair)
            pool.wait_ge(kv_d, 16 * 64)
            pool.wait_ge(at_pv, 33)
            st.link(g_.memset(smask[:], 0.0))
            st.link(g_.affine_select(out=smask[:], in_=smask[:], compare_op=ALU.is_ge, fill=NEG, base=0,
                                     pattern=[[0, 3], [-4, NS]], channel_multiplier=1))
            g_.affine_select(out=smask[:], in_=smask[:], compare_op=ALU.is_ge, fill=NEG, base=3,
                             pattern=[[0, 3], [4, NS]], channel_multiplier=-1).then_inc(masks_s, 1)
            for k in range(24):
                pool.wait_ge(m_h, k + 1)
                g_.tensor_tensor(m_lo[:, k // 3, tgc[k % 3]], pt[:, 2 * (k % 2) + 1, :],
                                 m_hi[:, k // 3, tgc[k % 3]].bitcast(F32), ALU.subtract).then_inc(m_l, 1)
            sums = 0

            def y1_square(m, tg):
                nonlocal sums
                pool.wait_ge(free[tg], M0["wo"] + m + 2)
                y = y1[:, m, tgc[tg]]
                if m == 0:
                    g_.tensor_tensor(acc[:, tg, :], y, y, ALU.mult).then_inc(y1_a, 1)
                else:
                    pool.wait_ge(y1_a, sums)
                    st.link(g_.tensor_tensor(sq[:, 0, :], y, y, ALU.mult))
                    g_.tensor_tensor(acc[:, tg, :], acc[:, tg, :], sq[:, 0, :], ALU.add).then_inc(y1_a, 1)
                sums += 1

            def x1_add(tg, ms):
                for m in ms:
                    k = 8 * tg + m
                    pool.wait_ge(x1_t, k + 1)
                    part = xT[:, m, tgc[tg]]
                    g_.tensor_tensor(part, part, nt_[:, k % 3, :], ALU.add).then_inc(x1_s, 1)

            for k in range(3 * WT):
                y1_square(k // 3, k % 3)
            for t in range(2):
                pool.wait_ge(xr_c[t], 9)
            for n in range(3):
                y1_square(WT + n % 2, n // 2)
            x1_add(0, range(0, 3))
            y1_square(WT + 1, 1)
            x1_add(0, range(3, 6))
            y1_square(WT, 2)
            x1_add(0, range(6, 8))
            y1_square(WT + 1, 2)

            def a_low(j, tg, g3):
                pool.wait_ge(ff_h, g3 + 1)
                g_.tensor_tensor(a_lo[:, j, tgc[tg]], sq[:, (3 * j + tg) % 2, :], a_hi[:, j, tgc[tg]].bitcast(F32),
                                 ALU.subtract).then_inc(ff_l, 1)

            for tg in range(3):
                if tg < 2:
                    x1_add(tg + 1, range(8))
                a_low(0, tg, tg)
            for j in range(1, FG):
                for tg in range(3):
                    a_low(j, tg, 3 * j + tg)
            with pool.Fori(1, ROUNDS) as i:
                for j in range(FG):
                    for tg in range(3):
                        a_low(j, tg, 12 * i + 3 * j + tg)
            for j in range(2):
                for tg in range(3):
                    a_low(j, tg, 12 * ROUNDS + 3 * j + tg)
            for k in range(24):
                pool.wait_ge(y2_q, k + 1)
                if k % 8 == 0:
                    g_.tensor_scalar(acc[:, k // 8, :], sq[:, k % 2, :], 1.0, 1.0, ALU.mult, ALU.mult).then_inc(y2_a, 1)
                else:
                    pool.wait_ge(y2_a, k)
                    g_.tensor_tensor(acc[:, k // 8, :], acc[:, k // 8, :], sq[:, k % 2, :], ALU.add).then_inc(y2_a, 1)
            for tg, m in [(0, m) for m in range(8)] + [(2, 6), (2, 7)]:
                pool.wait_ge(z_t, 8 * tg + m + 1)
                part = xT[:, m, tgc[tg]]
                g_.tensor_tensor(part, part, y2[:, m, tgc[tg]], ALU.add).then_inc(z_s[1], 1)


_INS = ["x_prompt", "x_sample", "cache_win0", "cache_win1", "cache_win2", "g_mix_pre", "g_mix_post", "g_ffn_pre",
        "g_ffn_post", "w_in", "ln_v_g", "ln_v_b", "w_sg", "b_sg", "w_proj_attn", "w_proj_sg", "w_out", "w_gate",
        "w_up", "w_down"]
_OUTS = [("y_prompt", (1, SEQ, D)), ("y_sample", (NS, 1, D)),
         ("kv_prompt_g0", (1, 1, 128, 2, 4, HD)), ("kv_prompt_g1", (1, 1, 512, 2, 4, HD)),
         ("kv_prompt_g2", (1, 1, 1024, 2, 4, HD)), ("kv_sample_g0", (1, NS, 1, 2, 4, HD)),
         ("kv_sample_g1", (1, NS, 1, 2, 4, HD)), ("kv_sample_g2", (1, NS, 1, 2, 4, HD)),
         ("sg_v_sample", (1, NS, 1, SGW))]


def kernel(**inputs):
    import numpy as _np
    import concourse.bacc as _bacc
    from concourse.bass_utils import run_bass_kernel_spmd as _run

    nc = _bacc.Bacc("TRN2", target_bir_lowering=False, num_devices=1)
    arrays, A, O = {}, {}, {}
    for name in _INS:
        a = _np.ascontiguousarray(inputs[name])
        arrays[f"in_{name}"] = a
        A[name] = nc.dram_tensor(f"in_{name}", a.shape, mybir.dt.from_np(a.dtype), kind="ExternalInput").ap()
    for name, shape in _OUTS:
        O[name] = nc.dram_tensor(f"out_{name}", shape, F32, kind="ExternalOutput").ap()
    build(nc, A, O)
    r = _run(nc, [arrays], core_ids=[0])
    return tuple(r.results[0][f"out_{name}"] for name, _ in _OUTS)
```
